# Optimizing a Trainium2 kernel written in Bass

```python
import math
import jax, jax.numpy as jnp
from jax import lax
import numpy as np

D_MODEL = 1024
BATCH = 1
SEQ = 256
DEPTH = 2

SSM_WIDTH = 256
SSM_GROUP = 16
SSM_GROUPS = SSM_WIDTH // SSM_GROUP
SSM_STATE = 64
HGRN_HEADS = 4
HGRN_DK = 64
HGRN_DV = 64
HGRN_WIDTH = HGRN_HEADS * HGRN_DV
HGRN_CHUNK = 64
ATT_HEADS = 8
ATT_HEAD_DIM = 64
ATT_WIDTH = ATT_HEADS * ATT_HEAD_DIM
ATT_Q_RANK = 256
ATT_KV_RANK = 128
IDX_HEADS = 4
IDX_DIM = 64
TOPK_MAX = 256
Q_BLOCK = 128
MASK_VALUE = -1e30
N_BRANCHES = 3
FFN_DENSE = 2816
N_EXPERTS = 8
TOP_K = 2
FFN_EXPERT = 3584
N_DENSE_LAYERS = (DEPTH + 1) // 2
N_MOE_LAYERS = DEPTH // 2
DEEPNORM_ALPHA = (2 * DEPTH) ** 0.25
DEEPNORM_BETA = (8 * DEPTH) ** -0.25
LN_EPS = 1e-5
RMS_EPS = 1e-6
F_MIN = 1e-12

IN_SPLITS = (SSM_WIDTH,
             HGRN_HEADS * HGRN_DK,
             HGRN_HEADS * HGRN_DK,
             HGRN_WIDTH,
             HGRN_WIDTH,
             ATT_Q_RANK,
             ATT_KV_RANK,
             IDX_DIM,
             IDX_HEADS,
             N_BRANCHES * D_MODEL)
N_IN = sum(IN_SPLITS)

kernel_name = 'hybrid_s5_hgrn2_dsa_deepnorm_moe'

def layer_norm(x, g, b):
    xf = x.astype(jnp.float32)
    mu = jnp.mean(xf, axis=-1, keepdims=True)
    var = jnp.mean(jnp.square(xf - mu), axis=-1, keepdims=True)
    return ((xf - mu) * lax.rsqrt(var + LN_EPS) * g + b).astype(x.dtype)

def rms_norm(x, g):
    xf = x.astype(jnp.float32)
    return (xf * lax.rsqrt(jnp.mean(xf * xf, axis=-1, keepdims=True) + RMS_EPS) * g).astype(x.dtype)

def swiglu(x, wg, wu, wd):
    return (jax.nn.silu(x @ wg) * (x @ wu)) @ wd

def _ssm_combine(e1, e2):
    a1r, a1i, b1r, b1i = e1
    a2r, a2i, b2r, b2i = e2
    return (a2r * a1r - a2i * a1i,
            a2r * a1i + a2i * a1r,
            a2r * b1r - a2i * b1i + b2r,
            a2r * b1i + a2i * b1r + b2i)

def s5_branch(u, log_dt, lam_re, lam_im, b_re, b_im, c_re, c_im, d_skip, w_glu, b_glu, w_out):
    f32 = jnp.float32
    bsz, seq, _ = u.shape
    uf = u.astype(f32)
    ug = uf.reshape(bsz, seq, SSM_GROUPS, SSM_GROUP)
    lre, lim = lam_re.astype(f32), lam_im.astype(f32)
    dt = jnp.exp(log_dt.astype(f32))[:, None]
    mag = jnp.exp(lre * dt)
    ang = lim * dt
    a_re, a_im = mag * jnp.cos(ang), mag * jnp.sin(ang)
    den = lre * lre + lim * lim
    coef_re = ((a_re - 1.0) * lre + a_im * lim) / den
    coef_im = (a_im * lre - (a_re - 1.0) * lim) / den
    br, bi = b_re.astype(f32), b_im.astype(f32)
    bb_re = coef_re[..., None] * br - coef_im[..., None] * bi
    bb_im = coef_re[..., None] * bi + coef_im[..., None] * br
    bu_re = jnp.einsum('bsgc,gpc->bsgp', ug, bb_re)
    bu_im = jnp.einsum('bsgc,gpc->bsgp', ug, bb_im)
    ar = jnp.broadcast_to(a_re, bu_re.shape)
    ai = jnp.broadcast_to(a_im, bu_re.shape)
    _, _, h_re, h_im = lax.associative_scan(_ssm_combine, (ar, ai, bu_re, bu_im), axis=1)
    y = (jnp.einsum('bsgp,gcp->bsgc', h_re, c_re.astype(f32))
         - jnp.einsum('bsgp,gcp->bsgc', h_im, c_im.astype(f32)))
    y = y.reshape(bsz, seq, SSM_WIDTH) + d_skip.astype(f32) * uf
    y = jax.nn.gelu(y)
    y = y * jax.nn.sigmoid(y @ w_glu.astype(f32) + b_glu.astype(f32))
    return y.astype(u.dtype) @ w_out

def hgrn2_branch(q, f_logit, i_in, g_out, lower_bound, norm_g, w_out):
    f32 = jnp.float32
    bsz, seq, _ = q.shape
    nc = seq // HGRN_CHUNK

    def heads(t, dim):
        return jnp.moveaxis(t.astype(f32).reshape(bsz, nc, HGRN_CHUNK, HGRN_HEADS, dim), 1, 0)

    z = f_logit.astype(f32)
    lb = lower_bound.astype(f32)
    f = lb + (1.0 - lb) * jax.nn.sigmoid(z)
    log_f = jnp.log(jnp.maximum(f, F_MIN))
    k_in = (1.0 - lb) * jax.nn.sigmoid(-z)
    qh, kh, vh = heads(q, HGRN_DK), heads(k_in, HGRN_DK), heads(i_in, HGRN_DV)
    bcum = jnp.cumsum(heads(log_f, HGRN_DK), axis=2)
    causal = jnp.tril(jnp.ones((HGRN_CHUNK, HGRN_CHUNK), dtype=bool))[None, :, :, None, None]

    def step(state, inp):
        qc, kc, vc, bc = inp
        o_inter = jnp.einsum('bthk,bhkv->bthv', qc * jnp.exp(bc), state)
        diff = bc[:, :, None] - bc[:, None, :]
        decay = jnp.where(causal, jnp.exp(jnp.where(causal, diff, 0.0)), 0.0)
        att = jnp.einsum('bthk,bshk,btshk->bhts', qc, kc, decay)
        o_intra = jnp.einsum('bhts,bshv->bthv', att, vc)
        b_last = bc[:, -1]
        state = (jnp.exp(b_last)[..., None] * state
                 + jnp.einsum('bshk,bshv->bhkv', kc * jnp.exp(b_last[:, None] - bc), vc))
        return state, o_inter + o_intra

    s0 = jnp.zeros((bsz, HGRN_HEADS, HGRN_DK, HGRN_DV), f32)
    _, o = lax.scan(step, s0, (qh, kh, vh, bcum))
    o = jnp.moveaxis(o, 0, 1).reshape(bsz, seq, HGRN_HEADS, HGRN_DV)
    o = rms_norm(o, norm_g).reshape(bsz, seq, HGRN_WIDTH) * jax.nn.silu(g_out.astype(f32))
    return o.astype(q.dtype) @ w_out

def dsa_branch(c_q, c_kv, k_idx, w_idx, q_norm_g, kv_norm_g, w_uq, w_qidx, w_ukv, w_out):
    f32 = jnp.float32
    bsz, seq, _ = c_q.shape
    n_sel = min(TOPK_MAX, seq // 4)
    cq = rms_norm(c_q, q_norm_g)
    ckv = rms_norm(c_kv, kv_norm_g)
    q = (cq @ w_uq).reshape(bsz, seq, ATT_HEADS, ATT_HEAD_DIM)
    q_idx = (cq @ w_qidx).reshape(bsz, seq, IDX_HEADS, IDX_DIM)
    kv = (ckv @ w_ukv).reshape(bsz, seq, 2, ATT_HEADS, ATT_HEAD_DIM)
    k, v = kv[:, :, 0], kv[:, :, 1]
    kid = k_idx.astype(f32)
    w = w_idx.astype(f32) * IDX_HEADS ** -0.5
    slopes = 2.0 ** (-8.0 * jnp.arange(1, ATT_HEADS + 1, dtype=f32) / ATT_HEADS)
    key_pos = jnp.arange(seq)
    nb = seq // Q_BLOCK

    def blocks(t):
        return jnp.moveaxis(t.reshape(bsz, nb, Q_BLOCK, *t.shape[2:]), 1, 0)

    def attend(inp):
        qb, qib, wb, start = inp
        q_pos = start + jnp.arange(Q_BLOCK)
        s_idx = jnp.einsum('bthd,bsd->bths', qib.astype(f32), kid) * IDX_DIM ** -0.5
        score = jnp.einsum('bths,bth->bts', jax.nn.relu(s_idx), wb)
        score = jnp.where(key_pos[None, None, :] <= q_pos[None, :, None], score, MASK_VALUE)
        _, sel = lax.top_k(score, n_sel)
        valid = sel <= q_pos[None, :, None]
        k_sel = jax.vmap(lambda kk, ii: kk[ii])(k, sel)
        v_sel = jax.vmap(lambda vv, ii: vv[ii])(v, sel)
        logits = jnp.einsum('bthd,btkhd->bthk', qb.astype(f32), k_sel.astype(f32)) * ATT_HEAD_DIM ** -0.5
        dist = (q_pos[None, :, None] - sel).astype(f32)
        logits = logits - slopes[None, None, :, None] * dist[:, :, None, :]
        logits = jnp.where(valid[:, :, None, :], logits, MASK_VALUE)
        p = jax.nn.softmax(logits, axis=-1)
        return jnp.einsum('bthk,btkhd->bthd', p, v_sel.astype(f32))

    starts = jnp.arange(nb) * Q_BLOCK
    o = lax.map(attend, (blocks(q), blocks(q_idx), blocks(w), starts))
    o = jnp.moveaxis(o, 0, 1).reshape(bsz, seq, ATT_WIDTH)
    return o.astype(c_q.dtype) @ w_out

def moe_ffn(x, router, wg, wu, wd):
    bsz, seq, d = x.shape
    xt = x.reshape(bsz * seq, d)
    logits = (xt @ router).astype(jnp.float32)
    top_val, top_idx = lax.top_k(logits, TOP_K)
    top_w = jax.nn.softmax(top_val, axis=-1)
    out = jnp.zeros((bsz * seq, d), jnp.float32)
    for e in range(N_EXPERTS):
        gate_e = jnp.sum(jnp.where(top_idx == e, top_w, 0.0), axis=-1)
        out = out + gate_e[:, None] * swiglu(xt, wg[e], wu[e], wd[e])
    return out.astype(x.dtype).reshape(bsz, seq, d)

def setup_inputs(seed: int = 0) -> dict:
    key = jax.random.key(seed)
    ks = jax.random.split(key, 40)
    f32 = jnp.float32

    def nrm(i, shape, scale):
        return jax.random.normal(ks[i], shape, f32) * scale

    G, P = SSM_GROUPS, SSM_STATE
    lam_im0 = jnp.broadcast_to(jnp.pi * jnp.arange(P, dtype=f32), (DEPTH, G, P))
    return {
        'x': nrm(0, (BATCH, SEQ, D_MODEL), 1.0),
        'w_in': nrm(1, (DEPTH, D_MODEL, N_IN), D_MODEL ** -0.5),
        'ssm_log_dt': jax.random.uniform(ks[2], (DEPTH, G), f32, math.log(1e-3), math.log(1e-1)),
        'ssm_lambda_re': -0.5 + nrm(3, (DEPTH, G, P), 0.01),
        'ssm_lambda_im': lam_im0 + nrm(4, (DEPTH, G, P), 0.01),
        'ssm_b_re': nrm(5, (DEPTH, G, P, SSM_GROUP), (2 * SSM_GROUP) ** -0.5),
        'ssm_b_im': nrm(6, (DEPTH, G, P, SSM_GROUP), (2 * SSM_GROUP) ** -0.5),
        'ssm_c_re': nrm(7, (DEPTH, G, SSM_GROUP, P), (2 * P) ** -0.5),
        'ssm_c_im': nrm(8, (DEPTH, G, SSM_GROUP, P), (2 * P) ** -0.5),
        'ssm_d': nrm(9, (DEPTH, SSM_WIDTH), 1.0),
        'ssm_w_glu': nrm(10, (DEPTH, SSM_WIDTH, SSM_WIDTH), SSM_WIDTH ** -0.5),
        'ssm_b_glu': nrm(11, (DEPTH, SSM_WIDTH), 0.01),
        'ssm_w_out': nrm(12, (DEPTH, SSM_WIDTH, D_MODEL), SSM_WIDTH ** -0.5 * DEEPNORM_BETA),
        'hgrn_lb_logits': nrm(13, (DEPTH, HGRN_HEADS * HGRN_DK), 1.0),
        'hgrn_norm_g': 1.0 + nrm(14, (DEPTH, HGRN_DV), 0.01),
        'hgrn_w_out': nrm(15, (DEPTH, HGRN_WIDTH, D_MODEL), HGRN_WIDTH ** -0.5 * DEEPNORM_BETA),
        'attn_q_norm_g': 1.0 + nrm(16, (DEPTH, ATT_Q_RANK), 0.01),
        'attn_kv_norm_g': 1.0 + nrm(17, (DEPTH, ATT_KV_RANK), 0.01),
        'attn_w_uq': nrm(18, (DEPTH, ATT_Q_RANK, ATT_WIDTH), ATT_Q_RANK ** -0.5),
        'attn_w_qidx': nrm(19, (DEPTH, ATT_Q_RANK, IDX_HEADS * IDX_DIM), ATT_Q_RANK ** -0.5),
        'attn_w_ukv': nrm(20, (DEPTH, ATT_KV_RANK, 2 * ATT_WIDTH), ATT_KV_RANK ** -0.5),
        'attn_w_out': nrm(21, (DEPTH, ATT_WIDTH, D_MODEL), ATT_WIDTH ** -0.5 * DEEPNORM_BETA),
        'w_o': nrm(22, (DEPTH, D_MODEL, D_MODEL), D_MODEL ** -0.5 * DEEPNORM_BETA),
        'ln_g': 1.0 + nrm(23, (DEPTH, 2, D_MODEL), 0.01),
        'ln_b': nrm(24, (DEPTH, 2, D_MODEL), 0.01),
        'ffn_w_gate': nrm(25, (N_DENSE_LAYERS, D_MODEL, FFN_DENSE), D_MODEL ** -0.5),
        'ffn_w_up': nrm(26, (N_DENSE_LAYERS, D_MODEL, FFN_DENSE), D_MODEL ** -0.5),
        'ffn_w_down': nrm(27, (N_DENSE_LAYERS, FFN_DENSE, D_MODEL), FFN_DENSE ** -0.5 * DEEPNORM_BETA),
        'moe_router': nrm(28, (N_MOE_LAYERS, D_MODEL, N_EXPERTS), D_MODEL ** -0.5),
        'moe_w_gate': nrm(29, (N_MOE_LAYERS, N_EXPERTS, D_MODEL, FFN_EXPERT), D_MODEL ** -0.5),
        'moe_w_up': nrm(30, (N_MOE_LAYERS, N_EXPERTS, D_MODEL, FFN_EXPERT), D_MODEL ** -0.5),
        'moe_w_down': nrm(31, (N_MOE_LAYERS, N_EXPERTS, FFN_EXPERT, D_MODEL), FFN_EXPERT ** -0.5 * DEEPNORM_BETA),
    }

def reference(x, w_in, ssm_log_dt, ssm_lambda_re, ssm_lambda_im, ssm_b_re, ssm_b_im, ssm_c_re, ssm_c_im,
              ssm_d, ssm_w_glu, ssm_b_glu, ssm_w_out, hgrn_lb_logits, hgrn_norm_g, hgrn_w_out,
              attn_q_norm_g, attn_kv_norm_g, attn_w_uq, attn_w_qidx, attn_w_ukv, attn_w_out, w_o,
              ln_g, ln_b, ffn_w_gate, ffn_w_up, ffn_w_down, moe_router, moe_w_gate, moe_w_up, moe_w_down):
    bsz, seq, _ = x.shape
    split_at = np.cumsum(IN_SPLITS)[:-1].tolist()
    lb_soft = jax.nn.softmax(hgrn_lb_logits.astype(jnp.float32), axis=0)
    lower_bounds = jnp.concatenate([jnp.zeros_like(lb_soft[:1]), jnp.cumsum(lb_soft[1:], axis=0)], axis=0)
    h = x
    for l in range(DEPTH):
        proj = h @ w_in[l]
        u, hq, hf, hi, hg, cq, ckv, kidx, widx, gates = jnp.split(proj, split_at, axis=-1)
        y_ssm = s5_branch(u, ssm_log_dt[l], ssm_lambda_re[l], ssm_lambda_im[l], ssm_b_re[l], ssm_b_im[l],
                          ssm_c_re[l], ssm_c_im[l], ssm_d[l], ssm_w_glu[l], ssm_b_glu[l], ssm_w_out[l])
        y_hg = hgrn2_branch(hq, hf, hi, hg, lower_bounds[l], hgrn_norm_g[l], hgrn_w_out[l])
        y_att = dsa_branch(cq, ckv, kidx, widx, attn_q_norm_g[l], attn_kv_norm_g[l],
                           attn_w_uq[l], attn_w_qidx[l], attn_w_ukv[l], attn_w_out[l])
        g = jax.nn.sigmoid(gates.astype(jnp.float32)).reshape(bsz, seq, N_BRANCHES, D_MODEL)
        mixed = g[:, :, 0] * y_ssm + g[:, :, 1] * y_hg + g[:, :, 2] * y_att
        mix_out = mixed.astype(h.dtype) @ w_o[l]
        h = layer_norm(DEEPNORM_ALPHA * h + mix_out, ln_g[l, 0], ln_b[l, 0])
        if l % 2 == 0:
            ffn = swiglu(h, ffn_w_gate[l // 2], ffn_w_up[l // 2], ffn_w_down[l // 2])
        else:
            ffn = moe_ffn(h, moe_router[l // 2], moe_w_gate[l // 2], moe_w_up[l // 2], moe_w_down[l // 2])
        h = layer_norm(DEEPNORM_ALPHA * h + ffn, ln_g[l, 1], ln_b[l, 1])
    return h


_drawn_inputs = setup_inputs


def setup_inputs(seed=0):
    import zlib

    import numpy as np

    out = dict(_drawn_inputs(seed))
    spreads = {}
    factors = {'ssm_log_dt': 49.672,
     'ssm_lambda_re': 64.0,
     'ssm_lambda_im': 51.256,
     'ssm_b_re': 64.0,
     'ssm_b_im': 64.0,
     'ssm_c_re': 64.0,
     'ssm_c_im': 62.32,
     'ssm_w_glu': 2.738,
     'ssm_b_glu': 25.764,
     'hgrn_norm_g': 8.0,
     'attn_q_norm_g': 5.484,
     'attn_kv_norm_g': 8.0}
    for name, (base, spread) in spreads.items():
        noise = np.random.default_rng([zlib.crc32(name.encode()), seed]).standard_normal(out[name].shape)
        drawn = base * np.exp(spread * noise) if base else spread * noise
        out[name] = __import__('jax').numpy.asarray(drawn.astype(out[name].dtype))
    for name, factor in factors.items():
        out[name] = (out[name] * factor).astype(out[name].dtype)
    return out
```

```python
import math
from contextlib import ExitStack

import concourse.bass as bass
from concourse import mybir

F32 = mybir.dt.float32
F32R = mybir.dt.float32r
I32 = mybir.dt.int32
U8 = mybir.dt.uint8
ALU = mybir.AluOpType
ACT = mybir.ActivationFunctionType
AX_X = mybir.AxisListType.X

P = 128
T, D, DEPTH = 256, 1024, 2
TB = T // P
KD = D // P
SSM_W, SSM_G, SSM_C, SSM_N = 256, 16, 16, 64
STILES = SSM_G * SSM_N // P
HG_H, HG_K = 4, 64
AH, AD = 8, 64
IH = 4
N_SEL = 64
MASK = -1e30
TAKEN = -3e38
FFN_D, FFN_E, NE = 2816, 3584, 8
ALPHA = (2 * DEPTH) ** 0.25
COL_Q, COL_F, COL_V, COL_G, COL_CQ, COL_KV, COL_GATE = 256, 512, 768, 1024, 1280, 1536, 1732
N_KVI = 128 + 64 + 4
SLOT = 2048
RAW, SPLIT = 6, 3
CAP = 128
MAGIC = 1.5 * 2.0 ** 23
TWO_PI = (6.28125, 0.0019350051879882812, 2 * math.pi - 6.28125 - 0.0019350051879882812)
CH_FFN = FFN_D // 256
GR_MOE = FFN_E // 512


def psum_plan():
    order = []

    def use(bank, *label):
        order.append((label, bank))

    for g in range(4):
        use(g, "xT", g)
    for l in range(DEPTH):
        for b, n in enumerate(("cq", "kvi", "u", "hq", "hf", "hv", "hg")):
            use(b, n, l)
        use(7, "bt", l), use(2, "cct", l)
        use(3, "cqT", l), use(0, "kviT", l)
        use(1, "gate", l, 0)
        use(2, "q", l, 0), use(3, "q", l, 1), use(4, "qi", l), use(5, "k", l, 0), use(6, "k", l, 1)
        use(7, "v", l, 0), use(0, "v", l, 1)
        use(1, "gate", l, 1)
        use(2, "idx", l, 0), use(3, "idx", l, 1), use(4, "idx", l, 2), use(7, "idx", l, 3)
        use(5, "gate", l, 2), use(6, "gate", l, 3), use(5, "gate", l, 4), use(6, "gate", l, 5)
        use(2, "lg", l, 0), use(3, "lg", l, 1)
        use(4, "lg", l, 2), use(7, "lg", l, 3), use(0, "lg", l, 4), use(1, "lg", l, 5)
        n = 0
        for lv in range(8):
            for odd in range(2):
                use((5, 6)[n % 2], "lev", l, lv, odd)
                n += 1
            if lv in (2, 4, 6):
                use(2, "gate", l, 5 + lv // 2)
        use(5, "lev", l, 8, 0), use(6, "lev", l, 8, 1)
        for i in range(6):
            use((7, 0)[i % 2], "pT", l, i)
            if i == 1:
                use(3, "o", l, 0)
        use(4, "o", l, 1)
        use(6, "ho", l)
        for pr in range(4):
            use((0, 2)[pr % 2], "bu", l, pr, 0), use((1, 3)[pr % 2], "bu", l, pr, 1)
            if pr == 0:
                use(5, "gate", l, 9)
            if pr == 1:
                use(7, "oT", l, 0), use(5, "oT", l, 1)
            if pr == 2:
                use(5, "hoT", l)
                use(5, "gate", l, 10)
        use(7, "gate", l, 11)
        use(4, "ssy", l)
        for q in range(4):
            use((5, 6)[q % 2], "y", l, 1, q)
        for q in range(4):
            use((5, 6)[q % 2], "y", l, 2, q)
        use(7, "glu", l)
        for q in range(4):
            use((5, 6)[q % 2], "y", l, 0, q)
        for c in range(4):
            use(c, "wo", l, c)
        for g in range(4):
            use(4 + g, "hT", l, 0, g)
        if l == 0:
            for tb in range(TB):
                for hf in range(2):
                    use(4 + 2 * tb + hf, "fd", tb, hf)
            for c in range(CH_FFN):
                use(c % 2, "fg", c), use(2 + c % 2, "fu", c)
            for g in range(4):
                use(g, "hT", l, 1, g)
        else:
            use(0, "router"), use(1, "rank")
    seen, plan = [0] * 8, {}
    for label, bank in order:
        assert label not in plan, label
        plan[label] = (bank, seen[bank])
        seen[bank] += 1
    return plan, seen


def hybrid_kernel(nc, x, w_in, log_dt, lam_re, lam_im, b_re, b_im, c_re, c_im, ssm_d, w_glu, b_glu, ssm_w_out,
                  lb_logits, hg_norm_g, hg_w_out, q_norm_g, kv_norm_g, w_uq, w_qidx, w_ukv, att_w_out, w_o,
                  ln_g, ln_b, ffn_gate, ffn_up, ffn_down, router, moe_gate, moe_up, moe_down, out):
    plan, bank_uses = psum_plan()

    jobs = []

    def tiles(src, r0, k, c0, n):
        return src[r0:r0 + k * P, c0:c0 + n].rearrange("(k p) n -> p k n", p=P)

    for l in range(DEPTH):
        for name, c0, n in (("cq", COL_CQ, 256), ("kvi", COL_KV, N_KVI), ("u", 0, 256), ("hq", COL_Q, 256),
                            ("hf", COL_F, 256), ("hv", COL_V, 256), ("hg", COL_G, 256)):
            jobs.append(((name, l), [(0, (KD, n), tiles(w_in[l], 0, KD, c0, n))]))

        def gate_job(c):
            jobs.append((("gate", l, c), [(0, (KD, 256), tiles(w_in[l], 0, KD, COL_GATE + 256 * c, 256))]))

        gate_job(0)
        jobs.append((("uq", l), [(0, (2, 512), tiles(w_uq[l], 0, 2, 0, 512)),
                                 (1024, (2, 256), tiles(w_qidx[l], 0, 2, 0, 256))]))
        jobs.append((("ukv", l), [(0, (1, 1024), tiles(w_ukv[l], 0, 1, 0, 1024))]))
        for c in range(1, 12):
            gate_job(c)
        jobs.append((("wout", l, 1), [(0, (2, D), tiles(hg_w_out[l], 0, 2, 0, D))]))
        for k in range(2):
            jobs.append((("wout", l, 2, k), [(0, (2, D), tiles(att_w_out[l], 2 * k * P, 2, 0, D))]))
        jobs.append((("glu", l), [(0, (2, 256), tiles(w_glu[l], 0, 2, 0, 256))]))
        jobs.append((("wout", l, 0), [(0, (2, D), tiles(ssm_w_out[l], 0, 2, 0, D))]))
        for c in range(4):
            jobs.append((("wo", l, c), [(0, (KD, 256), tiles(w_o[l], 0, KD, 256 * c, 256))]))
        if l == 0:
            for c in range(CH_FFN + 1):
                if c < CH_FFN:
                    jobs.append((("fg", c), [(0, (KD, 256), tiles(ffn_gate[0], 0, KD, 256 * c, 256))]))
                    jobs.append((("fu", c), [(0, (KD, 256), tiles(ffn_up[0], 0, KD, 256 * c, 256))]))
                if c > 0:
                    jobs.append((("fd", c - 1), [(0, (2, D), tiles(ffn_down[0], 256 * (c - 1), 2, 0, D))]))
    job_at = {name: n for n, (name, _) in enumerate(jobs)}
    full_value, filled = [], [0] * RAW
    for n, (_, parts) in enumerate(jobs):
        filled[n % RAW] += 16 * len(parts)
        full_value.append(filled[n % RAW])
    N_JOBS = len(jobs)
    split_names = [n for n, _ in jobs if n[0] in ("fg", "fu", "fd")]
    split_at = {name: m for m, name in enumerate(split_names)}
    N_SPLIT = len(split_names)

    moe_jobs = []
    for g in range(GR_MOE + 1):
        if g < GR_MOE:
            moe_jobs += [("g", g, 0), ("g", g, 1), ("u", g, 0), ("u", g, 1)]
        if g > 0:
            moe_jobs += [("d", g - 1, 0), ("d", g - 1, 1)]
    N_MOE = len(moe_jobs)
    moe_at = {name: j for j, name in enumerate(moe_jobs)}
    assert N_MOE % RAW == 0 and N_MOE % SPLIT == 0 and N_SPLIT % SPLIT == 0

    ctx = ExitStack()
    with ctx:
        arena = [nc.sbuf_base + (-nc.sbuf_base) % 32]

        def place(name, shape, dt, at):
            return nc.alloc_sbuf_tensor_at(name, shape, dt, offset=at).ap()

        def nbytes(shape, dt):
            n = 1 if dt == U8 else 4
            for s in shape[1:]:
                n *= s
            return n + (-n) % 32

        def sb(name, shape, dt=F32):
            at = arena[0]
            arena[0] += nbytes(shape, dt)
            return place(name, shape, dt, at)

        sems = {}

        def S(name):
            if name not in sems:
                sems[name] = ctx.enter_context(nc.semaphore(name))
            return sems[name]

        bank = [ctx.enter_context(nc.psum_tensor(f"bank{b}", [P, 512], F32))[:, :] for b in range(8)]
        raw_full = [S(f"raw_full{i}") for i in range(RAW)]
        bank_full = [S(f"bank_full{i}") for i in range(8)]
        bank_free = [S(f"bank_free{i}") for i in range(8)]

        raw = [sb(f"raw{i}", [P, SLOT]) for i in range(RAW)]
        h_t = sb("h_t", [P, TB, D])
        cos_t = sb("cos_t", [P, STILES, T])
        sin_t = sb("sin_t", [P, STILES, T])
        lng = sb("lng", [P, 2, D])
        ident = sb("ident", [P, P])
        negd = sb("negd", [P, 3 * P])
        lev_mask = sb("lev_mask", [P, 8, P], U8)
        tri = sb("tri", [P, P])
        ones = sb("ones", [P, P])
        jrow = sb("jrow", [P, P])
        pow_m = sb("pow_m", [P, 2])
        par = sb("par", [P, 2])
        par_i = sb("par_i", [P, 2], I32)
        ip = sb("ip", [P, P], I32)
        jf = sb("jf", [P, P], I32)
        lam = sb("lam", [P, 3, STILES])
        mag = sb("mag", [P, STILES])
        sc = sb("sc", [P, 16, STILES])
        wpow = sb("wpow", [P, 2, 8, STILES])
        bbT = sb("bbT", [P, 2, 2, P])
        ccT = sb("ccT", [P, 2, 2, P])
        scol = sb("scol", [P, 11])
        lbl = sb("lbl", [P, 2, 2])
        hgn = sb("hgn", [P, HG_K])
        stat = sb("stat", [P, 96])
        small_end = arena[0]

        hT = sb("hT", [P, KD, T])
        gates = sb("gates", [P, 24, T])
        cqs = sb("cqs", [P, TB, 512])
        o_at = place("o_at", [P, TB, 512], F32, arena[0] - 4096)
        qT = sb("qT", [P, 4, T])
        oT = place("oT", [P, 4, T], F32, arena[0] - 4096)
        cT = sb("cT", [P, 4, T])
        qiT = sb("qiT", [P, 2, T])
        kT = sb("kT", [P, 4, T])
        v_at = sb("v_at", [P, TB, 512])
        widx = sb("widx", [P, TB, IH])
        score = sb("score", [P, 3 * P])
        work = sb("work", [P, 3 * P])
        top8 = sb("top8", [P, 8])
        ssm_base = arena[0]
        prob = sb("prob", [P, 8 * 384])
        pT = sb("pT", [P, 2, 8, P])
        relu_s = place("relu_s", [P, 4 * 384], F32, ssm_base)
        xr = [place(f"xr{i}", [P, 2, T], F32, ssm_base + 2048 * i) for i in range(2)]
        xi = [place(f"xi{i}", [P, 2, T], F32, ssm_base + 4096 + 2048 * i) for i in range(2)]
        sv = [place(f"sv{i}", [P, 2, T], F32, ssm_base + 8192 + 2048 * i) for i in range(2)]
        hre = place("hre", [P, 2, T], F32, ssm_base + 12288)
        him = place("him", [P, 2, T], F32, ssm_base + 14336)
        sp_ = [place(f"sp{i}", [P, 2, T], F32, ssm_base + 16384 + 2048 * i) for i in range(2)]
        uT = sb("uT", [P, 2, T])
        tmp_at = arena[0]
        ys = sb("ys", [P, 2, T])
        yg = sb("yg", [P, 2, T])
        ysig = sb("ysig", [P, 2, T])
        hq = sb("hq", [P, 2, T])
        hk = sb("hk", [P, 2, T])
        hP = sb("hP", [P, 2, T])
        hR = sb("hR", [P, 2, T])
        lq = [sb(f"lq{i}", [P, 2, T]) for i in range(2)]
        lk = [sb(f"lk{i}", [P, 2, T]) for i in range(2)]
        h_att = sb("h_att", [P, 3, 4, P])
        hv = sb("hv", [P, TB, 256])
        hgs = sb("hgs", [P, TB, 256])
        ho = sb("ho", [P, TB, 256])
        hoT = sb("hoT", [P, 2, T])
        b_raw = sb("b_raw", [P, 2, STILES, SSM_C])
        mix_end = arena[0]

        arena[0] = small_end
        whi = [sb(f"whi{i}", [P, SLOT], F32R) for i in range(SPLIT)]
        wlo = [sb(f"wlo{i}", [P, SLOT], F32R) for i in range(SPLIT)]
        shared_end = arena[0]
        xh = sb("xh", [P, KD, T], F32R)
        xl = sb("xl", [P, KD, T], F32R)
        a_f = [sb(f"a_f{i}", [P, 2, T]) for i in range(2)]
        a_h = [sb(f"a_h{i}", [P, 2, T], F32R) for i in range(2)]
        a_l = [sb(f"a_l{i}", [P, 2, T], F32R) for i in range(2)]
        ffn_end = arena[0]
        arena[0] = shared_end
        ht_h = sb("ht_h", [P, TB, D], F32R)
        ht_l = sb("ht_l", [P, TB, D], F32R)
        xe_h = sb("xe_h", [P, KD, CAP], F32R)
        xe_l = sb("xe_l", [P, KD, CAP], F32R)
        ea = [sb(f"ea{i}", [P, 512]) for i in range(2)]
        et_h = [sb(f"et_h{i}", [P, 4, CAP], F32R) for i in range(2)]
        et_l = [sb(f"et_l{i}", [P, 4, CAP], F32R) for i in range(2)]
        y_e = sb("y_e", [P, D])
        sel = sb("sel", [P, TB, CAP], F32R)
        selg = sb("selg", [P, TB, CAP])
        selT = sb("selT", [P, TB, CAP])
        hTr = sb("hTr", [P, KD, T])
        wrt = sb("wrt", [P, KD, NE])
        rt = sb("rt", [P, 12, TB, NE])
        rs = sb("rs", [P, 10, TB])
        cur = sb("cur", [P, 4])
        over = sb("over", [P, 8])
        over_i = sb("over_i", [1, 1], I32)
        moe_end = arena[0]
        tab_tmp = [place("tab_tmp0", [P, STILES, P], F32, tmp_at), place("tab_tmp1", [P, STILES, P], F32, ffn_end)]
        c_raw = place("c_raw", [P, 2, 2, SSM_N], F32, ssm_base)
        c_exp = place("c_exp", [P, 2, 2, P], F32, ssm_base + 1024)
        b_exp = place("b_exp", [P, 2, STILES, 32], F32, ssm_base + 1024 + 2048)
        b_tmp = place("b_tmp", [P, 2, STILES, SSM_C], F32, ssm_base + 5120)
        assert max(mix_end, ffn_end, moe_end) <= nc.sbuf_usable_end

        MS, MEAN, RMS = stat[:, 0:4], stat[:, 4:8], stat[:, 8:12]
        bn6 = stat[:, 12:36].rearrange("p (b h s) -> p b h s", b=TB, h=2)
        mv = stat[:, 36:40].rearrange("p (b s) -> p b s", b=TB)
        rstd, veps = stat[:, 40:42], stat[:, 42:44]
        nmax, psumv = stat[:, 44:60], stat[:, 60:76]
        hss, hrr = stat[:, 76:84], stat[:, 84:92]
        prob0 = prob[:, 0:1024].rearrange("p (h s) -> p h s", h=AH)
        prob1 = prob[:, 1024:3072].rearrange("p (h s) -> p h s", h=AH)
        probs = [prob0, prob1]
        LAYER = lambda l: l + 1

        def wide(ap, shape):
            return ap.unsqueeze(len(ap.shape)).to_broadcast(shape)

        def full(eng, *label):
            b, n = plan[label]
            eng.wait_ge(bank_full[b], n + 1)
            return bank[b]

        def taken(eng, *label):
            b, n = plan[label]
            eng.wait_ge(bank_free[b], n + 1)

        def pT_part(i):
            hg, kb = i % 2, (0, 1, 0)[i // 2]
            return pT[:, kb, 4 * hg:4 * hg + 4, :]

        def pair(ap, pr):
            return ap.rearrange("p (m j) t -> p j m t", m=2)[:, pr]

        def by(n):
            return lambda b: b[:, :].rearrange("p (a n) -> p a n", n=n)

        class Link:

            def __init__(self, eng, name, start=0):
                self.eng, self.sem, self.n, self.start = eng, S(name), 0, start

            def __call__(self, ins):
                self.n += 1
                ins.then_inc(self.sem, 1)
                self.eng.wait_ge(self.sem, self.start + self.n)

        moe_order = [(("selT",), 6), (("xe", 0), 7), (("xe", 1), 6), (("xe", 2), 7), (("xe", 3), 6),
                     (("g", 0), 0), (("u", 0), 2)]
        for g in range(GR_MOE):
            if g + 1 < GR_MOE:
                moe_order.append((("g", g + 1), (g + 1) % 2))
            moe_order.append((("t", g), 7 if g % 2 == 0 else 6))
            if g + 1 < GR_MOE:
                moe_order.append((("u", g + 1), 2 + (g + 1) % 2))
            if g == 0:
                moe_order += [(("y", 0), 4), (("y", 1), 5)]
        moe_order += [(("sc", q), (7, 6)[q % 2]) for q in range(4)]
        moe_uses, moe_plan = [0] * 8, {}
        for label, b in moe_order:
            moe_plan[label] = (b, moe_uses[b])
            moe_uses[b] += 1

        def moe_bank(label, it):
            b, k = moe_plan[label]
            return b, bank_uses[b] + it * moe_uses[b] + k

        def moe_full(eng, it, *label):
            b, n = moe_bank(label, it)
            eng.wait_ge(bank_full[b], n + 1)
            return bank[b]

        def moe_slot(j):
            s = (N_JOBS + j) % RAW
            return s, j // RAW

        last_use = {"uq": ("qi",), "ukv": ("v", 1), "glu": ("glu",)}

        def released(eng, n):
            name = jobs[n][0]
            if name in split_at:
                eng.wait_ge(S("lo_full"), split_at[name] + 1)
                return
            kind, l = name[:2]
            label = name
            if kind == "wout":
                label = ("y", l, name[2], 3)
            elif kind in last_use:
                label = (last_use[kind][0], l) + last_use[kind][1:]
            full(eng, *label)

        PER_SLOT = N_MOE // RAW
        block = ctx.enter_context(nc.Block())

        @block.sync
        def _(sp):
            for tb in range(TB):
                sp.dma_start(h_t[:, tb, :], x[0, tb * P:(tb + 1) * P, :]).then_inc(S("x_in"), 16)
            for n, (name, parts) in enumerate(jobs):
                if n >= RAW:
                    released(sp, n - RAW)
                for at, (k, m), src in parts:
                    dst = raw[n % RAW][:, at:at + k * m].rearrange("p (k n) -> p k n", k=k)
                    sp.dma_start(dst, src).then_inc(raw_full[n % RAW], 16)

            def experts(first):
                with sp.Fori(0, NE) as e:
                    it = e + first
                    for j, (kind, g, hf) in enumerate(moe_jobs):
                        s, turn = moe_slot(j)
                        sp.wait_ge(S("lo_full"), it * N_MOE + (N_SPLIT + j - RAW + 1))
                        if kind == "d":
                            src = moe_down[0][bass.ds(e, 1)][:, 512 * g + 256 * hf:512 * g + 256 * hf + 256, :]
                        else:
                            w = moe_gate if kind == "g" else moe_up
                            src = w[0][bass.ds(e, 1)][:, 512 * hf:512 * hf + 512, 512 * g:512 * g + 512]
                        src = src.rearrange("e (k p) n -> p (e k) n", p=P)
                        dst = raw[s][:, :].rearrange("p (k n) -> p k n", k=src.shape[1])
                        sp.dma_start(dst, src).then_inc(raw_full[s], 16)

            for n in range(N_JOBS - RAW, N_JOBS):
                released(sp, n)
            experts(0)
            sp.wait_ge(S("over_ready"), 1)
            with sp.If(sp.value_load(over_i[0:1, 0:1], min_val=0, max_val=T) > CAP):
                experts(NE)
            for tb in range(TB):
                sp.wait_ge(S("h_ready"), 2 * (2 * DEPTH - 1) + tb + 1)
                sp.dma_start(out[0, tb * P:(tb + 1) * P, :], h_t[:, tb, :]).then_inc(S("stored"), 16)
            sp.wait_ge(S("stored"), 32)

        @block.gpsimd
        def _(pool):
            link = Link(pool, "pool_link")
            pool.memset(ident, 0.0).then_inc(S("c0"), 1)
            pool.memset(ones, 1.0).then_inc(S("c0"), 1)
            pool.memset(tri, 1.0).then_inc(S("c0"), 1)
            pool.memset(pow_m[:, 0:1], -0.5).then_inc(S("c0"), 1)
            pool.memset(pow_m[:, 1:2], -1.0).then_inc(S("c0"), 1)
            pool.iota(ip, pattern=[[0, P]], base=0, channel_multiplier=1).then_inc(S("c0"), 1)
            pool.iota(jf, pattern=[[1, P]], base=0, channel_multiplier=0).then_inc(S("c0"), 1)
            pool.iota(jrow, pattern=[[1, P]], base=0, channel_multiplier=0,
                      allow_small_or_imprecise_dtypes=True).then_inc(S("c0"), 1)
            pool.iota(negd[:, 0:P], pattern=[[1, P]], base=0, channel_multiplier=-1,
                      allow_small_or_imprecise_dtypes=True).then_inc(S("c0"), 1)
            pool.iota(negd[:, P:3 * P], pattern=[[1, T]], base=-P, channel_multiplier=-1,
                      allow_small_or_imprecise_dtypes=True).then_inc(S("c0"), 1)
            pool.wait_ge(S("c0"), 10)
            pool.affine_select(out=ident, in_=ident, compare_op=ALU.not_equal, fill=1.0, base=0,
                               pattern=[[-1, P]], channel_multiplier=1).then_inc(S("consts"), 1)
            pool.affine_select(out=tri, in_=tri, compare_op=ALU.is_gt, fill=0.0, base=0,
                               pattern=[[1, P]], channel_multiplier=-1).then_inc(S("consts"), 1)
            for part in (negd[:, 0:P], negd[:, 2 * P:3 * P]):
                pool.affine_select(out=part, in_=part, compare_op=ALU.is_ge, fill=MASK, base=0,
                                   pattern=[[-1, P]], channel_multiplier=1).then_inc(S("consts"), 1)

            def tables(l):
                pool.dma_start(lam[:, 0, :], lam_re[l].rearrange("(j g) p -> (g p) j", g=2), allow_slow_non_contiguous=True).then_inc(S("lam_in"), 16)
                pool.dma_start(lam[:, 1, :], lam_im[l].rearrange("(j g) p -> (g p) j", g=2), allow_slow_non_contiguous=True).then_inc(S("lam_in"), 16)
                for g in range(2):
                    pool.dma_start(lam[64 * g:64 * g + 64, 2, :],
                                   log_dt[l:l + 1].rearrange("o (j g) -> o g j", g=2)[:, g, :].to_broadcast((64, STILES)), allow_slow_non_contiguous=True).then_inc(S("lam_in"), 16)
                pool.wait_ge(S("dt"), LAYER(l))
                pool.tensor_tensor(sc[:, 1, :], lam[:, 0, :], sc[:, 0, :], ALU.mult).then_inc(S("expo"), 1)
                link(pool.tensor_tensor(sc[:, 2, :], lam[:, 1, :], sc[:, 0, :], ALU.mult))
                link(pool.tensor_scalar(sc[:, 3, :], sc[:, 2, :], 1 / (2 * math.pi), MAGIC, ALU.mult, ALU.add))
                link(pool.tensor_scalar(sc[:, 3, :], sc[:, 3, :], -MAGIC, 1.0, ALU.add, ALU.mult))
                for c in TWO_PI:
                    link(pool.tensor_scalar(sc[:, 4, :], sc[:, 3, :], -c, 0.0, ALU.mult, ALU.add))
                    link(pool.tensor_tensor(sc[:, 2, :], sc[:, 4, :], sc[:, 2, :], ALU.add))
                link(pool.tensor_scalar(sc[:, 4, :], sc[:, 2, :], 3.1415925, -3.1415925, ALU.min, ALU.max))
                pool.tensor_scalar(sc[:, 5, :], sc[:, 4, :], 0.5, 0.0, ALU.mult, ALU.add).then_inc(S("angle"), 1)
                pool.wait_ge(S("sines"), 2 * LAYER(l))
                link(pool.tensor_tensor(sc[:, 8, :], sc[:, 7, :], sc[:, 7, :], ALU.mult))
                link(pool.tensor_scalar(sc[:, 8, :], sc[:, 8, :], -2.0, 1.0, ALU.mult, ALU.add))
                pool.wait_ge(S("mag"), LAYER(l))
                link(pool.tensor_tensor(sc[:, 9, :], mag, sc[:, 8, :], ALU.mult))
                link(pool.tensor_tensor(sc[:, 10, :], mag, sc[:, 6, :], ALU.mult))
                link(pool.tensor_scalar(sc[:, 11, :], sc[:, 9, :], -1.0, 1.0, ALU.add, ALU.mult))
                link(pool.tensor_tensor(sc[:, 12, :], lam[:, 0, :], lam[:, 0, :], ALU.mult))
                link(pool.tensor_tensor(sc[:, 13, :], lam[:, 1, :], lam[:, 1, :], ALU.mult))
                link(pool.tensor_tensor(sc[:, 12, :], sc[:, 12, :], sc[:, 13, :], ALU.add))
                link(pool.tensor_tensor(sc[:, 12, :], sc[:, 12, :], pow_m[:, 1:2].to_broadcast((P, STILES)), ALU.pow))
                link(pool.tensor_tensor(sc[:, 13, :], sc[:, 11, :], lam[:, 0, :], ALU.mult))
                link(pool.tensor_tensor(sc[:, 14, :], sc[:, 10, :], lam[:, 1, :], ALU.mult))
                link(pool.tensor_tensor(sc[:, 13, :], sc[:, 13, :], sc[:, 14, :], ALU.add))
                link(pool.tensor_tensor(sc[:, 13, :], sc[:, 13, :], sc[:, 12, :], ALU.mult))
                link(pool.tensor_tensor(sc[:, 14, :], sc[:, 10, :], lam[:, 0, :], ALU.mult))
                link(pool.tensor_tensor(sc[:, 15, :], sc[:, 11, :], lam[:, 1, :], ALU.mult))
                link(pool.tensor_tensor(sc[:, 14, :], sc[:, 14, :], sc[:, 15, :], ALU.subtract))
                link(pool.tensor_tensor(sc[:, 14, :], sc[:, 14, :], sc[:, 12, :], ALU.mult))

            def rotations(l):
                pool.memset(cos_t[:, :, 0:1], 1.0)
                pool.memset(sin_t[:, :, 0:1], 0.0)
                link(pool.tensor_copy(wpow[:, 0, 0, :], sc[:, 8, :]))
                link(pool.tensor_copy(wpow[:, 1, 0, :], sc[:, 6, :]))
                for i in range(8):
                    n = 1 << i
                    wc = wide(wpow[:, 0, i, :], (P, STILES, n))
                    ws = wide(wpow[:, 1, i, :], (P, STILES, n))
                    c0, s0, c1, s1 = cos_t[:, :, 0:n], sin_t[:, :, 0:n], cos_t[:, :, n:2 * n], sin_t[:, :, n:2 * n]
                    t0 = tab_tmp[l][:, :, 0:n]
                    pool.tensor_tensor(c1, c0, wc, ALU.mult)
                    link(pool.tensor_tensor(t0, s0, ws, ALU.mult))
                    link(pool.tensor_tensor(c1, c1, t0, ALU.subtract))
                    pool.tensor_tensor(s1, c0, ws, ALU.mult)
                    link(pool.tensor_tensor(t0, s0, wc, ALU.mult))
                    link(pool.tensor_tensor(s1, s1, t0, ALU.add))
                    if i < 7:
                        link(pool.tensor_tensor(sc[:, 8, :], wpow[:, 1, i, :], wpow[:, 1, i, :], ALU.mult))
                        link(pool.tensor_tensor(wpow[:, 0, i + 1, :], wpow[:, 0, i, :], wpow[:, 0, i, :], ALU.mult))
                        link(pool.tensor_tensor(wpow[:, 0, i + 1, :], wpow[:, 0, i + 1, :], sc[:, 8, :], ALU.subtract))
                        link(pool.tensor_tensor(sc[:, 8, :], wpow[:, 0, i, :], wpow[:, 1, i, :], ALU.mult))
                        link(pool.tensor_scalar(wpow[:, 1, i + 1, :], sc[:, 8, :], 2.0, 0.0, ALU.mult, ALU.add))
                pool.sem_inc(S("tables"), 1)

            def load_norm(n):
                l, j = divmod(n, 2)
                if n > 0:
                    pool.wait_ge(S("h_ready"), 2 * n)
                pool.dma_start(lng[:, 0, :], ln_g[l, j:j + 1, :].to_broadcast((P, D))).then_inc(S("norm_in"), 16)
                pool.dma_start(lng[:, 1, :], ln_b[l, j:j + 1, :].to_broadcast((P, D))).then_inc(S("norm_in"), 16)

            def rsqrt(dst, src, tmp, scale, eps):
                link(pool.tensor_scalar(tmp, src, scale, eps, ALU.mult, ALU.add))
                return pool.tensor_tensor(dst, tmp, pow_m[:, 0:1].to_broadcast(tuple(dst.shape)), ALU.pow)

            def norm(n):
                pool.wait_ge(S("norm_var"), n + 1)
                rsqrt(rstd, mv[:, :, 1], veps, 1.0, 1e-5).then_inc(S("norm_rstd"), 1)

            tables(0)
            for l in range(DEPTH):
                L = LAYER(l)
                if l > 0:
                    pool.wait_ge(S("h_ready"), 4 * l)
                for ri, src in enumerate((b_re, b_im)):
                    pool.dma_start(b_raw[:, ri], src[l].rearrange("(j g) p c -> (g p) j c", g=2)).then_inc(S("bc_in"), 16)
                for ri, src in enumerate((c_re, c_im)):
                    pool.dma_start(c_raw[:, ri], src[l].rearrange("(m g) c p -> (g c) m p", m=2)).then_inc(S("bc_in"), 16)
                cols = [(0, ssm_d[l]), (2, b_glu[l]), (4, q_norm_g[l])]
                for c, src in cols:
                    pool.dma_start(scol[:, c:c + 2], src.rearrange("(m p) -> p m", p=P), allow_slow_non_contiguous=True).then_inc(S("col_in"), 16)
                pool.dma_start(scol[:, 6:7], kv_norm_g[l].rearrange("(m p) -> p m", p=P), allow_slow_non_contiguous=True).then_inc(S("col_in"), 16)
                for i in range(2):
                    pool.dma_start(lbl[:, i, :], lb_logits[i].rearrange("(m p) -> p m", p=P), allow_slow_non_contiguous=True).then_inc(S("col_in"), 16)
                pool.dma_start(hgn, hg_norm_g[l:l + 1, :].to_broadcast((P, HG_K))).then_inc(S("col_in"), 16)
                load_norm(2 * l)
                pool.memset(b_exp, 0.0)
                pool.memset(h_att, 0.0).then_inc(S("h_att_zero"), 1)
                for b in range(2):
                    pool.memset(lq[b], 0.0).then_inc(S("lev_zero"), 1)
                    link(pool.memset(lk[b], 0.0))
                pool.wait_ge(S("par"), 1)
                pool.wait_ge(S("bc_in"), 64 * L)
                cre = wide(sc[:, 13, :], (P, STILES, SSM_C))
                cim = wide(sc[:, 14, :], (P, STILES, SSM_C))
                for ri, (w0, w1, op) in enumerate(((cre, cim, ALU.subtract), (cim, cre, ALU.add))):
                    pool.tensor_tensor(b_tmp[:, 0], b_raw[:, 0], w0, ALU.mult)
                    link(pool.tensor_tensor(b_tmp[:, 1], b_raw[:, 1], w1, ALU.mult))
                    for g in range(2):
                        r = slice(64 * g, 64 * g + 64)
                        ins = pool.tensor_tensor(b_exp[r, ri, :, SSM_C * g:SSM_C * (g + 1)], b_tmp[r, 0], b_tmp[r, 1], op)
                        if g == 0 or ri == 0:
                            link(ins)
                        else:
                            ins.then_inc(S("b_exp_ready"), 1)
                pool.wait_ge(S("b_exp_ready"), L)
                for ri in range(2):
                    for g in range(2):
                        pool.tensor_scalar(c_exp[:, ri, :, 64 * g:64 * g + 64], c_raw[:, ri], par[:, g:g + 1], 1.0,
                                           ALU.mult, ALU.mult).then_inc(S("c_exp"), 1)

                pool.wait_ge(S("squares"), 4 * L)
                pool.tensor_scalar(MEAN[:, 0:2], MS[:, 0:2], 1.0 / 256, 1e-6, ALU.mult, ALU.add)
                link(pool.tensor_scalar(MEAN[:, 2:4], MS[:, 2:4], 1.0 / 128, 1e-6, ALU.mult, ALU.add))
                pool.tensor_tensor(RMS, MEAN, pow_m[:, 0:1].to_broadcast((P, 4)), ALU.pow).then_inc(S("rms"), 1)
                if l == 0:
                    rotations(0)
                pool.wait_ge(S("ho_sum"), L)
                rsqrt(hrr, hss, hss, 1.0 / HG_K, 1e-6).then_inc(S("ho_rms"), 1)
                for pr in range(4):
                    ct, st = pair(cos_t, pr), pair(sin_t, pr)
                    gr, gi = xr[pr % 2], xi[pr % 2]
                    pool.wait_ge(S("scan"), 4 * (4 * l + pr + 1))
                    if pr > 0:
                        pool.wait_ge(S("states_used"), 3 * l + pr)
                    pool.tensor_tensor(hre, gr, ct, ALU.mult)
                    link(pool.tensor_tensor(sp_[0], gi, st, ALU.mult))
                    pool.tensor_tensor(him, gr, st, ALU.mult)
                    pool.tensor_tensor(sp_[1], gi, ct, ALU.mult).then_inc(S("scan_used"), 1)
                    pool.tensor_tensor(hre, hre, sp_[0], ALU.subtract).then_inc(S("states"), 1)
                    pool.wait_ge(S("scan_used"), 4 * l + pr + 1)
                    pool.tensor_tensor(him, him, sp_[1], ALU.add).then_inc(S("states"), 1)
                taken(pool, "ssy", l)
                link(pool.tensor_tensor(yg, ys, ys, ALU.mult))
                link(pool.tensor_scalar(yg, yg, 0.044715, 1.0, ALU.mult, ALU.add))
                pool.tensor_tensor(yg, yg, ys, ALU.mult).then_inc(S("gelu_in"), 1)
                pool.wait_ge(S("gelu_sig"), L)
                pool.tensor_tensor(yg, ys, ysig, ALU.mult).then_inc(S("gelu"), 1)
                taken(pool, "glu", l)
                pool.wait_ge(S("gelu"), L)
                pool.tensor_tensor(ys, yg, ysig, ALU.mult).then_inc(S("ssm_out"), 1)
                norm(2 * l)
                if l == 0:
                    pool.wait_ge(S("h_ready"), 2)
                    load_norm(1)
                    tables(1)
                    rotations(1)
                    norm(1)
                else:
                    load_norm(2 * l + 1)
                    pool.dma_start(wrt, router[0].rearrange("(k p) e -> p k e", p=P)).then_inc(S("router_in"), 16)
            norm(2 * DEPTH - 1)

        @block.scalar
        def _(act):
            link = Link(act, "act_link")

            def evac(dst, label, part=None, last=True, func=ACT.Copy, scale=1.0, bias=0.0):
                src = full(act, *label)
                src = src if part is None else part(src)
                ins = act.activation(dst, src, func, scale=scale, bias=bias)
                if last:
                    ins.then_inc(bank_free[plan[label][0]], 1)
                return ins

            def ssm_exps(l):
                act.wait_ge(S("lam_in"), 64 * LAYER(l))
                act.activation(sc[:, 0, :], lam[:, 2, :], ACT.Exp).then_inc(S("dt"), 1)
                act.wait_ge(S("expo"), LAYER(l))
                act.activation(mag, sc[:, 1, :], ACT.Exp).then_inc(S("mag"), 1)
                act.wait_ge(S("angle"), LAYER(l))
                act.activation(sc[:, 6, :], sc[:, 4, :], ACT.Sin).then_inc(S("sines"), 1)
                act.activation(sc[:, 7, :], sc[:, 5, :], ACT.Sin).then_inc(S("sines"), 1)

            def hi(name):
                n, m = job_at[name], split_at[name]
                act.wait_ge(raw_full[n % RAW], full_value[n])
                if m >= SPLIT:
                    act.wait_ge(S("split_free"), m - SPLIT + 1)
                act.activation(whi[m % SPLIT], raw[n % RAW], ACT.Copy).then_inc(S("hi_full"), 1)

            for g in range(4):
                tb, kk = divmod(g, 2)
                evac(hT[:, 4 * kk:4 * kk + 4, tb * P:(tb + 1) * P], ("xT", g), by(P))
            ssm_exps(0)
            for l in range(DEPTH):
                L = LAYER(l)
                for tb in range(TB):
                    act.activation(hre[:, tb, :], by(256)(full(act, "cq", l))[:, tb, :], ACT.Square,
                                   accum_out=MS[:, tb:tb + 1]).then_inc(S("squares"), 1)
                for tb in range(TB):
                    act.activation(him[:, tb, 0:128], by(256)(full(act, "kvi", l))[:, tb, 0:128], ACT.Square,
                                   accum_out=MS[:, 2 + tb:3 + tb]).then_inc(S("squares"), 1)
                for r in range(2):
                    evac(cqs[:, :, 384 + 64 * r:448 + 64 * r], ("kvi", l), lambda b: by(256)(b)[:, :, 128:192], last=False)
                act.activation(widx, by(256)(full(act, "kvi", l))[:, :, 192:196], ACT.Copy,
                               scale=IH ** -0.5 * 64 ** -0.5).then_inc(S("kid"), 1)
                evac(uT, ("u", l), by(256))
                evac(hq, ("hq", l), by(256))
                evac(hP, ("hf", l), by(256), last=False, func=ACT.Sigmoid)
                evac(hk, ("hf", l), by(256), func=ACT.Sigmoid, scale=-1.0)
                if l > 0:
                    act.wait_ge(S("lb_diff"), 1)
                    act.activation(scol[:, 7:9], lbl[:, 1, :], ACT.Sigmoid).then_inc(S("lb_sig"), 1)
                evac(hv, ("hv", l), by(256))
                act.activation(hgs, by(256)(full(act, "hg", l)), ACT.Sigmoid).then_inc(S("hg_sig"), 1)
                evac(bbT.rearrange("p a b n -> p (a b n)"), ("bt", l))
                evac(ccT[:, 0].rearrange("p b n -> p (b n)"), ("cct", l), lambda b: b[:, 0:256], last=False)
                evac(ccT[:, 1].rearrange("p b n -> p (b n)"), ("cct", l), lambda b: b[:, 256:512], scale=-1.0)
                act.wait_ge(S("col_in"), 112 * L)
                for f in range(2):
                    evac(cT[:, f, :], ("cqT", l), lambda b: b[:, 256 * f:256 * f + 256], last=f == 1,
                         scale=scol[:, 4 + f:5 + f])
                evac(cT[:, 2, :], ("kviT", l), lambda b: b[:, 0:256], last=False, scale=scol[:, 6:7])
                evac(cT[:, 3, :], ("kviT", l), lambda b: b[:, 256:512])

                def gate(c):
                    evac(gates[:, 2 * c:2 * c + 2, :], ("gate", l, c), by(256), func=ACT.Sigmoid)

                gate(0)
                for i in range(2):
                    evac(qT[:, 2 * i:2 * i + 2, :], ("q", l, i), by(256), scale=AD ** -0.5)
                evac(qiT, ("qi", l), by(256))
                for i in range(2):
                    evac(kT[:, 2 * i:2 * i + 2, :], ("k", l, i), by(256))
                for tb in range(TB):
                    evac(v_at[:, tb, :], ("v", l, tb))
                gate(1)
                for i in range(4):
                    n = 2 * P if i < 2 else 2 * T
                    o = 256 * i if i < 2 else 512 * (i - 1)
                    evac(relu_s[:, o:o + n], ("idx", l, i), lambda b: b[:, 0:n], func=ACT.Relu)
                for c in range(2, 6):
                    gate(c)
                for tb in range(TB):
                    act.wait_ge(S("row_max"), 2 * l + tb + 1)
                    for h in range(AH):
                        c = tb * AH + h
                        act.activation(probs[tb][:, h, :], probs[tb][:, h, :], ACT.Exp, bias=nmax[:, c:c + 1],
                                       accum_out=psumv[:, c:c + 1]).then_inc(S("probs"), 1)
                for c in range(6, 9):
                    gate(c)
                act.wait_ge(S("h_att_zero"), L)
                for odd in range(2):
                    evac(h_att[:, 2].rearrange("p (a odd) t -> p a odd t", odd=2)[:, :, odd, :], ("lev", l, 8, odd),
                         lambda b: by(P)(b)[:, 0:2, :])
                for i in (0, 2, 4):
                    if i == 4:
                        full(act, "o", l, 0)
                    evac(pT_part(i), ("pT", l, i), by(P))
                act.activation(lq[0].rearrange("p a n -> p (a n)"), full(act, "ho", l), ACT.Square).then_inc(S("ho_sq"), 1)
                gate(9)
                for i in range(2):
                    evac(oT[:, 2 * i:2 * i + 2, :], ("oT", l, i), by(256))
                evac(hoT, ("hoT", l), by(256))
                gate(10)
                gate(11)
                act.wait_ge(S("gelu_in"), L)
                act.activation(ysig, yg, ACT.Sigmoid, scale=2 * math.sqrt(2 / math.pi)).then_inc(S("gelu_sig"), 1)
                for m in range(2):
                    src = full(act, "glu", l)[:, 256 * m:256 * m + 256]
                    if m == 0:
                        act.wait_ge(S("gelu"), L)
                    ins = act.activation(ysig[:, m, :], src, ACT.Sigmoid, bias=scol[:, 2 + m:3 + m])
                ins.then_inc(bank_free[plan[("glu", l)][0]], 1)
                if l == 0:
                    for g in range(4):
                        tb, kk = divmod(g, 2)
                        act.activation(xh[:, 4 * kk:4 * kk + 4, tb * P:(tb + 1) * P], by(P)(full(act, "hT", 0, 0, g)),
                                       ACT.Copy).then_inc(S("xh"), 1)
                    ssm_exps(1)
                    hi(("fg", 0)), hi(("fu", 0))
                    for c in range(CH_FFN):
                        if c + 1 < CH_FFN:
                            hi(("fg", c + 1)), hi(("fu", c + 1))
                        act.activation(a_f[c % 2].rearrange("p a n -> p (a n)"), full(act, "fg", c), ACT.Silu
                                       ).then_inc(bank_free[c % 2], 1)
                        hi(("fd", c))
                        taken(act, "fu", c)
                        act.activation(a_h[c % 2], a_f[c % 2], ACT.Copy).then_inc(S("ffn_ah"), 1)
                    for g in range(4):
                        tb, kk = divmod(g, 2)
                        evac(hT[:, 4 * kk:4 * kk + 4, tb * P:(tb + 1) * P], ("hT", 0, 1, g), by(P))
                else:
                    for g in range(4):
                        tb, kk = divmod(g, 2)
                        evac(hTr[:, 4 * kk:4 * kk + 4, tb * P:(tb + 1) * P], ("hT", 1, 0, g), by(P))
                    for tb in range(TB):
                        act.activation(ht_h[:, tb, :], h_t[:, tb, :], ACT.Copy).then_inc(S("ht_h"), 1)
                    act.wait_ge(S("top_diff"), 1)
                    act.activation(rs[:, 6, :], rs[:, 5, :], ACT.Exp).then_inc(S("top_exp"), 1)

            def experts(first):
                with act.Fori(0, NE) as e:
                    it = e + first

                    def hi_e(*name):
                        j = moe_at[name]
                        s, turn = moe_slot(j)
                        act.wait_ge(raw_full[s], it * (16 * PER_SLOT) + (filled[s] + 16 * (turn + 1)))
                        act.wait_ge(S("split_free"), it * N_MOE + (N_SPLIT + j - SPLIT + 1))
                        act.activation(whi[(N_SPLIT + j) % SPLIT], raw[s], ACT.Copy).then_inc(S("hi_full"), 1)

                    def evac_e(dst, *label, src=lambda b: b[:, :], func=ACT.Copy, frees=True):
                        b, n = moe_bank(label, it)
                        ins = act.activation(dst, src(moe_full(act, it, *label)), func)
                        ins.then_inc(bank_free[b] if frees else S("et_h"), 1)

                    evac_e(selT, "selT", src=lambda b: b[:, 0:TB * P].rearrange("p (a n) -> p a n", n=P))
                    evac_e(xe_h[:, 0:4, :], "xe", 0, src=by(P))
                    evac_e(xe_l[:, 0:4, :], "xe", 2, src=by(P))
                    for half in range(2):
                        hi_e("g", 0, half)
                    for half in range(2):
                        hi_e("u", 0, half)
                    for g in range(GR_MOE):
                        if g + 1 < GR_MOE:
                            hi_e("g", g + 1, 0), hi_e("g", g + 1, 1)
                        evac_e(ea[g % 2], "g", g, func=ACT.Silu)
                        if g + 1 < GR_MOE:
                            hi_e("u", g + 1, 0), hi_e("u", g + 1, 1)
                        evac_e(et_h[g % 2], "t", g, src=by(P), frees=False)
                        hi_e("d", g, 0), hi_e("d", g, 1)
                    evac_e(y_e[:, 0:512], "y", 0)

            experts(0)
            act.wait_ge(S("over_ready"), 1)
            with act.If(act.value_load(over_i[0:1, 0:1], min_val=0, max_val=T) > CAP):
                experts(NE)

        @block.tensor
        def _(pe):
            owed = []

            def mm(dst, lhs, rhs, start, stop):
                ins = pe.matmul(dst, lhs, rhs, start=start, stop=stop)
                if owed:
                    ins.then_inc(S("split_free"), 1)
                    owed.clear()
                return ins

            def bank_for(*label):
                b, n = plan[label]
                if n > 0:
                    pe.wait_ge(bank_free[b], n)
                return bank[b]

            def done(ins, *label):
                ins.then_inc(bank_full[plan[label][0]], 1)

            def chunk(name):
                n = job_at[name]
                pe.wait_ge(raw_full[n % RAW], full_value[n])
                return raw[n % RAW]

            def by_token(name, label, n, lhs):
                w = chunk(name)[:, 0:KD * n].rearrange("p (k n) -> p k n", k=KD)
                b = bank_for(*label)
                for tb in range(TB):
                    for k in range(KD):
                        ins = mm(b[:, 256 * tb:256 * tb + n], lhs[:, k, tb * P:(tb + 1) * P], w[:, k, :],
                                 k == 0, k == KD - 1)
                done(ins, *label)

            def by_column(name, label):
                w = chunk(name).rearrange("p (k n) -> p k n", k=KD)
                b = bank_for(*label)
                for m in range(2):
                    for k in range(KD):
                        ins = mm(b[:, 256 * m:256 * m + 256], w[:, k, m * P:(m + 1) * P], hT[:, k, :],
                                 k == 0, k == KD - 1)
                done(ins, *label)

            def transposes(label, sources):
                b = bank_for(*label)
                for i, src in enumerate(sources):
                    ins = pe.transpose(b[0:src.shape[1], i * P:(i + 1) * P], src, ident)
                done(ins, *label)

            pe.wait_ge(S("consts"), 4)
            pe.wait_ge(S("x_in"), 32)
            for g in range(4):
                tb, kk = divmod(g, 2)
                transposes(("xT", g), [h_t[:, tb, P * k:P * (k + 1)] for k in range(4 * kk, 4 * kk + 4)])
            for l in range(DEPTH):
                L = LAYER(l)
                if l == 0:
                    for g in range(4):
                        taken(pe, "xT", g)
                else:
                    for g in range(4):
                        taken(pe, "hT", 0, 1, g)

                def gate(c):
                    by_column(("gate", l, c), ("gate", l, c))

                for name, n in (("cq", 256), ("kvi", N_KVI)):
                    by_token((name, l), (name, l), n, hT)
                for name in ("u", "hq", "hf"):
                    by_column((name, l), (name, l))
                for name in ("hv", "hg"):
                    by_token((name, l), (name, l), 256, hT)
                pe.wait_ge(S("b_exp_ready"), L)
                transposes(("bt", l), [b_exp[:, ri, 4 * m:4 * m + 4, :].rearrange("p j c -> p (j c)")
                                       for ri in range(2) for m in range(2)])
                pe.wait_ge(S("c_exp"), 4 * L)
                transposes(("cct", l), [c_exp[:, ri, m, :] for ri in range(2) for m in range(2)])
                taken(pe, "cq", l)
                taken(pe, "kvi", l)
                transposes(("cqT", l), [cqs[:, tb, P * f:P * f + P] for f in range(2) for tb in range(TB)])
                transposes(("kviT", l), [cqs[:, tb, P * f:P * f + P] for f in range(2, 4) for tb in range(TB)])
                gate(0)
                taken(pe, "cqT", l)
                w = chunk(("uq", l))
                uq, qidx = w[:, 0:1024].rearrange("p (k n) -> p k n", k=2), w[:, 1024:1536].rearrange("p (k n) -> p k n", k=2)
                for i in range(3):
                    label = ("q", l, i) if i < 2 else ("qi", l)
                    b = bank_for(*label)
                    for m in range(2):
                        for k in range(2):
                            lhs = uq[:, k, P * (2 * i + m):P * (2 * i + m + 1)] if i < 2 else qidx[:, k, P * m:P * m + P]
                            ins = mm(b[:, 256 * m:256 * m + 256], lhs, cT[:, k, :], k == 0, k == 1)
                    done(ins, *label)
                taken(pe, "kviT", l)
                ukv = chunk(("ukv", l))
                for i in range(2):
                    b = bank_for("k", l, i)
                    for m in range(2):
                        ins = mm(b[:, 256 * m:256 * m + 256], ukv[:, P * (2 * i + m):P * (2 * i + m + 1)], cT[:, 2, :],
                                 True, True)
                    done(ins, "k", l, i)
                for tb in range(TB):
                    ins = mm(bank_for("v", l, tb)[:, :], cT[:, 2, tb * P:(tb + 1) * P], ukv[:, 512:1024], True, True)
                    done(ins, "v", l, tb)
                gate(1)
                taken(pe, "qi", l)

                def head(ap, h):
                    return ap[64 * (h % 2):64 * (h % 2) + 64, h // 2]

                for i in range(4):
                    b = bank_for("idx", l, i)
                    tb, odd = divmod(i, 2)
                    keys = P * (tb + 1)
                    for j in range(2):
                        ins = mm(b[:, keys * j:keys * (j + 1)], head(qiT, 2 * j + odd)[:, tb * P:(tb + 1) * P],
                                 cT[64 * odd:64 * odd + 64, 3, 0:keys], True, True)
                    done(ins, "idx", l, i)
                for c in range(2, 6):
                    gate(c)
                taken(pe, "k", l, 1)
                for i in range(6):
                    b = bank_for("lg", l, i)
                    for j in range(4 if i < 2 else 2):
                        h = 2 * j + i if i < 2 else 4 * ((i - 2) // 2) + 2 * j + i % 2
                        keys, tb = (P, 0) if i < 2 else (T, 1)
                        ins = mm(b[:, keys * j:keys * (j + 1)], head(qT, h)[:, tb * P:(tb + 1) * P],
                                 head(kT, h)[:, 0:keys], True, True)
                    done(ins, "lg", l, i)
                for lv in range(9):
                    pe.wait_ge(S("lev_qk"), 9 * l + lv + 1)
                    q_, k_ = (hq, hk) if lv == 0 else (lq[lv % 2], lk[lv % 2])
                    for odd in range(2):
                        b = bank_for("lev", l, lv, odd)
                        for a in range(4 if lv < 8 else 2):
                            h = 2 * (a % 2) + odd
                            qb, kb = (a // 2, a // 2) if lv < 8 else (1, 0)
                            ins = mm(b[:, P * a:P * a + P], head(k_, h)[:, kb * P:(kb + 1) * P],
                                     head(q_, h)[:, qb * P:(qb + 1) * P], True, True)
                        done(ins, "lev", l, lv, odd)
                    if lv in (2, 4, 6):
                        gate(5 + lv // 2)
                for i in range(6):
                    pe.wait_ge(S("probs"), 16 * l + (8 if i < 2 else 16))
                    tb, kb, hg = (0, 0, i) if i < 2 else (1, (1, 0)[i // 2 - 1], i % 2)
                    transposes(("pT", l, i), [probs[tb][:, 4 * hg + j, kb * P:(kb + 1) * P] for j in range(4)])
                    if i == 1:
                        for n in range(2):
                            taken(pe, "pT", l, n)
                        b = bank_for("o", l, 0)
                        for h in range(AH):
                            ins = mm(b[:, AD * h:AD * h + AD], pT[:, 0, h, :], v_at[:, 0, AD * h:AD * h + AD], True, True)
                        done(ins, "o", l, 0)
                for n in range(2, 6):
                    taken(pe, "pT", l, n)
                b = bank_for("o", l, 1)
                for h in range(AH):
                    for kb in (0, 1):
                        ins = mm(b[:, AD * h:AD * h + AD], pT[:, kb, h, :], v_at[:, kb, AD * h:AD * h + AD],
                                 kb == 0, kb == 1)
                done(ins, "o", l, 1)
                taken(pe, "lev", l, 8, 0)
                taken(pe, "lev", l, 8, 1)
                taken(pe, "lev", l, 7, 0)
                taken(pe, "lev", l, 7, 1)
                b = bank_for("ho", l)
                for tb in range(TB):
                    for h in range(HG_H):
                        dst = b[:, 256 * tb + 64 * h:256 * tb + 64 * h + 64]
                        if tb == 1:
                            mm(dst, h_att[:, 2, h, :], hv[:, 0, 64 * h:64 * h + 64], True, False)
                        ins = mm(dst, h_att[:, tb, h, :], hv[:, tb, 64 * h:64 * h + 64], tb == 0, True)
                done(ins, "ho", l)
                def ssm_in(pr):
                    for ri in range(2):
                        b = bank_for("bu", l, pr, ri)
                        rows = slice(32 * pr, 32 * pr + 32)
                        for m in range(2):
                            ins = pe.matmul(b[:, 256 * m:256 * m + 256], bbT[rows, ri, m, :], uT[rows, m, :],
                                            start=True, stop=True, tile_position=(32 * pr, 0))
                        done(ins, "bu", l, pr, ri)

                def ssm_out(pr):
                    pe.wait_ge(S("states"), 2 * (4 * l + pr + 1))
                    b = bank[plan[("ssy", l)][0]] if pr > 0 else bank_for("ssy", l)
                    rows = slice(32 * pr, 32 * pr + 32)
                    for m in range(2):
                        for ri, st in enumerate((hre, him)):
                            ins = pe.matmul(b[rows, 256 * m:256 * m + 256], ccT[:, ri, m, rows], st[:, m, :],
                                            start=(ri == 0), stop=(ri == 1), tile_position=(0, 32 * pr))
                    ins.then_inc(S("states_used") if pr < 3 else bank_full[plan[("ssy", l)][0]], 1)

                ssm_in(0)
                gate(9)
                ssm_in(1)
                taken(pe, "o", l, 1)
                for i in range(2):
                    transposes(("oT", l, i), [o_at[:, tb, P * f:P * f + P] for f in (2 * i, 2 * i + 1) for tb in range(TB)])
                ssm_out(0)
                ssm_in(2)
                pe.wait_ge(S("ho_ready"), L)
                transposes(("hoT", l), [ho[:, tb, P * f:P * f + P] for f in range(2) for tb in range(TB)])
                gate(10)
                ssm_out(1)
                ssm_in(3)
                gate(11)

                def y_out(br, src, names):
                    w = [chunk(n).rearrange("p (k n) -> p k n", k=2) for n in names]
                    nk = 2 * len(names)
                    for q in range(4):
                        b = bank_for("y", l, br, q)
                        for m in range(2):
                            for k in range(nk):
                                ins = mm(b[:, 256 * m:256 * m + 256],
                                         w[k // 2][:, k % 2, P * (2 * q + m):P * (2 * q + m + 1)], src[:, k, :],
                                         k == 0, k == nk - 1)
                        done(ins, "y", l, br, q)

                taken(pe, "hoT", l)
                y_out(1, hoT, [("wout", l, 1)])
                ssm_out(2)
                taken(pe, "oT", l, 1)
                y_out(2, oT, [("wout", l, 2, 0), ("wout", l, 2, 1)])
                ssm_out(3)
                pe.wait_ge(S("gelu"), L)
                w = chunk(("glu", l))[:, 0:512].rearrange("p (k n) -> p k n", k=2)
                b = bank_for("glu", l)
                for m in range(2):
                    for k in range(2):
                        ins = mm(b[:, 256 * m:256 * m + 256], w[:, k, P * m:P * m + P], yg[:, k, :], k == 0, k == 1)
                done(ins, "glu", l)
                pe.wait_ge(S("ssm_out"), L)
                y_out(0, ys, [("wout", l, 0)])
                pe.wait_ge(S("mixed"), 4 * L)
                for c in range(4):
                    by_token(("wo", l, c), ("wo", l, c), 256, gates)
                for g in range(4):
                    tb, kk = divmod(g, 2)
                    pe.wait_ge(S("h_ready"), 4 * l + tb + 1)
                    transposes(("hT", l, 0, g), [h_t[:, tb, P * k:P * (k + 1)] for k in range(4 * kk, 4 * kk + 4)])
                if l == 0:
                    for g in range(4):
                        taken(pe, "hT", 0, 0, g)

                    def split_chunk(name):
                        m = split_at[name]
                        pe.wait_ge(S("lo_full"), m + 1)
                        return whi[m % SPLIT], wlo[m % SPLIT]

                    def up(kind, c):
                        wh, wl = (w.rearrange("p (k n) -> p k n", k=KD) for w in split_chunk((kind, c)))
                        b = bank_for(kind, c)
                        for m in range(2):
                            for k in range(KD):
                                dst, cs = b[:, 256 * m:256 * m + 256], slice(m * P, (m + 1) * P)
                                mm(dst, wh[:, k, cs], xh[:, k, :], k == 0, False)
                                mm(dst, wh[:, k, cs], xl[:, k, :], False, False)
                                ins = mm(dst, wl[:, k, cs], xh[:, k, :], False, k == KD - 1)
                        done(ins, kind, c)
                        owed.append(1)

                    def down(c):
                        pe.wait_ge(S("ffn_al"), c + 1)
                        wh, wl = (w.rearrange("p (k n) -> p k n", k=2) for w in split_chunk(("fd", c)))
                        for tb in range(TB):
                            for hf in range(2):
                                b = bank_for("fd", tb, hf) if c == 0 else bank[4 + 2 * tb + hf]
                                for k in range(2):
                                    ts, ds = slice(tb * P, (tb + 1) * P), slice(512 * hf, 512 * hf + 512)
                                    mm(b[:, :], a_h[c % 2][:, k, ts], wh[:, k, ds], c == 0 and k == 0, False)
                                    mm(b[:, :], a_l[c % 2][:, k, ts], wh[:, k, ds], False, False)
                                    ins = mm(b[:, :], a_h[c % 2][:, k, ts], wl[:, k, ds], False,
                                             c == CH_FFN - 1 and k == 1)
                                if c == CH_FFN - 1:
                                    done(ins, "fd", tb, hf)
                        owed.append(1)

                    up("fg", 0), up("fu", 0)
                    for c in range(CH_FFN):
                        if c + 1 < CH_FFN:
                            up("fg", c + 1), up("fu", c + 1)
                        down(c)
                    for g in range(4):
                        tb, kk = divmod(g, 2)
                        pe.wait_ge(S("h_ready"), 2 + tb + 1)
                        transposes(("hT", 0, 1, g), [h_t[:, tb, P * k:P * (k + 1)] for k in range(4 * kk, 4 * kk + 4)])
                    owed.clear()
                    pe.sem_inc(S("split_free"), 1)
                else:
                    for g in range(4):
                        taken(pe, "hT", 1, 0, g)
                    pe.wait_ge(S("router_in"), 16)
                    b = bank_for("router")
                    for tb in range(TB):
                        for k in range(KD):
                            ins = mm(b[:, NE * tb:NE * tb + NE], hTr[:, k, tb * P:(tb + 1) * P], wrt[:, k, :],
                                     k == 0, k == KD - 1)
                    done(ins, "router")
                    pe.wait_ge(S("routed"), 1)
                    b = bank_for("rank")
                    mm(b[:, 0:NE], tri, rt[:, 4, 0, :], True, True)
                    mm(b[:, NE:2 * NE], ones, rt[:, 4, 0, :], True, False)
                    mm(b[:, NE:2 * NE], tri, rt[:, 4, 1, :], False, True)
                    mm(b[:, 2 * NE:3 * NE], ones, rt[:, 4, 0, :], True, False)
                    done(mm(b[:, 2 * NE:3 * NE], ones, rt[:, 4, 1, :], False, True), "rank")

            def experts(first):
                with pe.Fori(0, NE) as e:
                    it = e + first

                    def room(*label):
                        b, n = moe_bank(label, it)
                        pe.wait_ge(bank_free[b], n)
                        return bank[b]

                    def done_e(ins, *label):
                        ins.then_inc(bank_full[moe_plan[label][0]], 1)

                    def taken_e(*label):
                        b, n = moe_bank(label, it)
                        pe.wait_ge(bank_free[b], n + 1)

                    def halves(*name):
                        j = moe_at[name]
                        pe.wait_ge(S("lo_full"), it * N_MOE + (N_SPLIT + j + 1))
                        m = (N_SPLIT + j) % SPLIT
                        return whi[m], wlo[m]

                    pe.wait_ge(S("sel"), it + 1)
                    b = room("selT")
                    for tb in range(TB):
                        ins = pe.transpose(b[:, tb * P:(tb + 1) * P], selg[:, tb, :], ident)
                    done_e(ins, "selT")
                    for i in range(4):
                        src, kk = (ht_h, ht_l)[i // 2], 4 * (i % 2)
                        b = room("xe", i)
                        for k in range(4):
                            for tb in range(TB):
                                ins = mm(b[:, P * k:P * k + CAP], src[:, tb, P * (kk + k):P * (kk + k + 1)],
                                         sel[:, tb, :], tb == 0, tb == TB - 1)
                        done_e(ins, "xe", i)

                    def up(kind, g):
                        b = room(kind, g)
                        for half in range(2):
                            wh, wl = (w.rearrange("p (k n) -> p k n", k=4) for w in halves(kind, g, half))
                            for k in range(4):
                                x_h, x_l = xe_h[:, 4 * half + k, :], xe_l[:, 4 * half + k, :]
                                first_, last_ = half == 0 and k == 0, half == 1 and k == 3
                                mm(b[0:CAP, :], x_h, wh[:, k, :], first_, False)
                                mm(b[0:CAP, :], x_l, wh[:, k, :], False, False)
                                ins = mm(b[0:CAP, :], x_h, wl[:, k, :], False, last_)
                            if half == 1:
                                done_e(ins, kind, g)
                            owed.append(1)

                    def down(g):
                        taken_e("t", g)
                        ys_ = [room("y", i) for i in range(2)] if g == 0 else [bank[4], bank[5]]
                        for half in range(2):
                            wh, wl = (w.rearrange("p (k n) -> p k n", k=2) for w in halves("d", g, half))
                            for i in range(2):
                                for k in range(2):
                                    eh, el = et_h[g % 2][:, 2 * half + k, :], et_l[g % 2][:, 2 * half + k, :]
                                    cs = slice(512 * i, 512 * i + 512)
                                    first_ = g == 0 and half == 0 and k == 0
                                    last_ = g == GR_MOE - 1 and half == 1 and k == 1
                                    mm(ys_[i][0:CAP, :], eh, wh[:, k, cs], first_, False)
                                    mm(ys_[i][0:CAP, :], el, wh[:, k, cs], False, False)
                                    ins = mm(ys_[i][0:CAP, :], eh, wl[:, k, cs], False, last_)
                                if g == GR_MOE - 1 and half == 1:
                                    done_e(ins, "y", i)
                            owed.append(1)

                    for i in range(4):
                        taken_e("xe", i)
                    up("g", 0), up("u", 0)
                    for g in range(GR_MOE):
                        if g + 1 < GR_MOE:
                            up("g", g + 1)
                        taken_e("u", g)
                        b = room("t", g)
                        for f in range(4):
                            ins = pe.transpose(b[:, P * f:P * f + CAP], ea[g % 2][:, P * f:P * f + P], ident)
                        done_e(ins, "t", g)
                        if g + 1 < GR_MOE:
                            up("u", g + 1)
                        down(g)
                    taken_e("y", 0), taken_e("y", 1)
                    for q in range(4):
                        tb, hf = divmod(q, 2)
                        b = room("sc", q)
                        ins = pe.matmul(b[:, :], selT[:, tb, :], y_e[:, 512 * hf:512 * hf + 512], start=True, stop=True)
                        done_e(ins, "sc", q)
                    owed.clear()
                    pe.sem_inc(S("split_free"), 1)

            experts(0)
            pe.wait_ge(S("over_ready"), 1)
            with pe.If(pe.value_load(over_i[0:1, 0:1], min_val=0, max_val=T) > CAP):
                experts(NE)

        @block.vector
        def _(dve):
            link = Link(dve, "dve_link")

            dve.wait_ge(S("c0"), 10)
            lev, below, cmp_ = score[:, 0:P], score[:, P:2 * P], work[:, 0:P]
            link(dve.tensor_copy(par_i, ip[:, 0:2]))
            link(dve.tensor_tensor(cmp_, jf, ip, ALU.is_gt))
            link(dve.tensor_tensor(ip, ip, jf, ALU.bitwise_xor))
            link(dve.tensor_copy(lev, ip))
            link(dve.tensor_scalar(lev_mask[:, 0, :], lev, 0.0, None, ALU.is_equal))
            link(dve.tensor_tensor(lev, lev, cmp_, ALU.mult))
            for j in range(7):
                link(dve.tensor_scalar(below, lev, float(2 << j), None, ALU.is_lt))
                link(dve.scalar_tensor_tensor(lev_mask[:, j + 1, :], lev, float(1 << j), below, ALU.is_ge, ALU.mult))
            link(dve.tensor_scalar(par_i, par_i, 4, 1, ALU.logical_shift_right, ALU.bitwise_and))
            link(dve.tensor_copy(par[:, 1:2], par_i[:, 0:1]))
            dve.tensor_scalar(par[:, 0:1], par[:, 1:2], -1.0, 1.0, ALU.mult, ALU.add).then_inc(S("par"), 1)
            link(dve.memset(scol[:, 7:9], 0.0))
            link(dve.memset(scol[:, 9:11], 1.0))

            def taken_by(b_label, ins):
                ins.then_inc(bank_free[plan[b_label][0]], 1)
                taken(dve, *b_label)

            def lo(name):
                n, m = job_at[name], split_at[name]
                dve.wait_ge(S("hi_full"), m + 1)
                dve.tensor_tensor(wlo[m % SPLIT], raw[n % RAW], whi[m % SPLIT].bitcast(F32), ALU.subtract
                                  ).then_inc(S("lo_full"), 1)

            def layer_norm(n):
                for tb in range(TB):
                    for hf in range(2):
                        link(dve.bn_stats(bn6[:, tb, hf, :], h_t[:, tb, 512 * hf:512 * hf + 512]))
                for tb in range(TB):
                    ins = dve.bn_aggr(mv[:, tb, :], bn6[:, tb])
                ins.then_inc(S("norm_var"), 1)
                dve.wait_ge(S("norm_rstd"), n + 1)
                dve.wait_ge(S("norm_in"), 32 * (n + 1))
                dve.wait_ge(S("norm_var"), n + 1)
                for tb in range(TB):
                    link(dve.tensor_scalar(h_t[:, tb, :], h_t[:, tb, :], mv[:, tb, 0:1], rstd[:, tb:tb + 1],
                                           ALU.subtract, ALU.mult))
                    link(dve.tensor_tensor(h_t[:, tb, :], h_t[:, tb, :], lng[:, 0, :], ALU.mult))
                    dve.tensor_tensor(h_t[:, tb, :], h_t[:, tb, :], lng[:, 1, :], ALU.add).then_inc(S("h_ready"), 1)

            def flat(ap):
                return ap.rearrange("p a t -> p (a t)")

            for l in range(DEPTH):
                L = LAYER(l)
                dve.wait_ge(S("rms"), L)
                dve.wait_ge(S("kid"), L)
                cqb, kvb = by(256)(full(dve, "cq", l)), by(256)(full(dve, "kvi", l))
                for tb in range(TB):
                    ins = dve.tensor_scalar(cqs[:, tb, 0:256], cqb[:, tb, :], RMS[:, tb:tb + 1], None, ALU.mult)
                ins.then_inc(bank_free[plan[("cq", l)][0]], 1)
                for tb in range(TB):
                    ins = dve.tensor_scalar(cqs[:, tb, 256:384], kvb[:, tb, 0:128], RMS[:, 2 + tb:3 + tb], None, ALU.mult)
                ins.then_inc(bank_free[plan[("kvi", l)][0]], 1)
                if l > 0:
                    dve.wait_ge(S("col_in"), 112 * L)
                    dve.tensor_tensor(lbl[:, 1, :], lbl[:, 1, :], lbl[:, 0, :], ALU.subtract).then_inc(S("lb_diff"), 1)
                    dve.wait_ge(S("lb_sig"), 1)
                    link(dve.tensor_scalar(scol[:, 9:11], scol[:, 7:9], -1.0, 1.0, ALU.mult, ALU.add))
                taken(dve, "hf", l)
                for m in range(2):
                    link(dve.tensor_scalar(hP[:, m, :], hP[:, m, :], scol[:, 9 + m:10 + m], scol[:, 7 + m:8 + m],
                                           ALU.mult, ALU.add))
                    link(dve.tensor_scalar(hk[:, m, :], hk[:, m, :], scol[:, 9 + m:10 + m], None, ALU.mult))
                link(dve.tensor_scalar(hP, hP, 1e-12, None, ALU.max))
                taken(dve, "hq", l)
                dve.memset(hR, 1.0).then_inc(S("lev_qk"), 1)
                dve.wait_ge(S("hg_sig"), L)
                ins = dve.tensor_tensor(hgs, hgs, by(256)(full(dve, "hg", l)), ALU.mult)
                taken_by(("hg", l), ins)
                dve.wait_ge(S("col_in"), 112 * L)
                hgs8 = hgs.rearrange("p b (h k) -> p (b h) k", k=HG_K)
                link(dve.tensor_tensor(hgs8, hgs8, hgn.unsqueeze(1).to_broadcast((P, 8, HG_K)), ALU.mult))
                dve.wait_ge(S("consts"), 4)
                for tb in range(TB):
                    n = P * (tb + 1)
                    o = P * tb
                    sco, wk, neg = score[:, o:o + n], work[:, o:o + n], negd[:, o:o + n]
                    for h in range(IH):
                        if h < 2:
                            taken(dve, "idx", l, 2 * tb + h)
                        o_h = (h % 2) * 2 * n + (h // 2) * n + 512 * tb
                        src = relu_s[:, o_h:o_h + n]
                        if h == 0:
                            link(dve.tensor_scalar(sco, src, widx[:, tb, 0:1], None, ALU.mult))
                        else:
                            link(dve.scalar_tensor_tensor(sco, src, widx[:, tb, h:h + 1], sco, ALU.mult, ALU.add))
                    link(dve.tensor_scalar(wk, neg, -1e29, MASK, ALU.is_lt, ALU.mult))
                    link(dve.tensor_tensor(sco, sco, wk, ALU.add))
                    src = sco
                    for r in range(N_SEL // 8):
                        link(dve.max(top8, src))
                        link(dve.match_replace(wk, top8, src, TAKEN))
                        src = wk
                    link(dve.tensor_scalar(sco, wk, TAKEN, MASK, ALU.not_equal, ALU.mult))
                    link(dve.tensor_tensor(sco, sco, neg, ALU.add))
                for tb in range(TB):
                    n, o = P * (tb + 1), P * tb
                    for h in range(AH):
                        i, j = (h % 2, h // 2) if tb == 0 else (2 + 2 * (h // 4) + h % 2, h % 4 // 2)
                        label = ("lg", l, i)
                        src = by(n)(full(dve, *label))[:, j, :]
                        ins = dve.scalar_tensor_tensor(probs[tb][:, h, :], score[:, o:o + n], 2.0 ** -(h + 1.0), src,
                                                       ALU.mult, ALU.add)
                        if j == 512 // n - 1:
                            ins.then_inc(bank_free[plan[label][0]], 1)
                    taken(dve, *label)
                    mx = nmax[:, 8 * tb:8 * tb + 8]
                    link(dve.tensor_reduce(mx, probs[tb], AX_X, ALU.max))
                    dve.tensor_scalar(mx, mx, -1.0, None, ALU.mult).then_inc(S("row_max"), 1)
                dve.wait_ge(S("lev_zero"), 2 * L)
                dve.wait_ge(S("h_att_zero"), L)

                def level(lv):
                    n = 1 << (lv - 1)
                    v4 = lambda ap: flat(ap).rearrange("p (b two n) -> p b two n", two=2, n=n)
                    q4, k4, P4, R4 = v4(hq), v4(hk), v4(hP), v4(hR)
                    nb = 512 // (2 * n)
                    dve.tensor_tensor(v4(lq[lv % 2])[:, :, 1, :], q4[:, :, 1, :], P4[:, :, 1, :], ALU.mult)
                    link(dve.tensor_tensor(v4(lk[lv % 2])[:, :, 0, :], k4[:, :, 0, :], R4[:, :, 0, :], ALU.mult))
                    if lv < 8:
                        link(dve.tensor_tensor(R4[:, :, 0, :], R4[:, :, 0, :],
                                               P4[:, :, 1, n - 1:n].to_broadcast((P, nb, n)), ALU.mult))
                        dve.tensor_tensor(P4[:, :, 1, :], P4[:, :, 1, :],
                                          P4[:, :, 0, n - 1:n].to_broadcast((P, nb, n)), ALU.mult
                                          ).then_inc(S("lev_qk"), 1)
                    else:
                        dve.sem_inc(S("lev_qk"), 1)
                    dve.wait_ge(S("lev_qk"), 9 * l + lv + 1)

                for lv in range(8):
                    level(lv + 1)
                    for odd in range(2):
                        dst = h_att[:, 0:2].rearrange("p b (a odd) t -> p (b a) odd t", odd=2)[:, :, odd, :]
                        mask = lev_mask[:, lv, :].unsqueeze(1).to_broadcast((P, 4, P))
                        ins = dve.copy_predicated(dst, mask, by(P)(full(dve, "lev", l, lv, odd)))
                        ins.then_inc(bank_free[plan[("lev", l, lv, odd)][0]], 1)
                for i in (1, 3, 5):
                    if i == 5:
                        full(dve, "o", l, 0)
                    ins = dve.tensor_copy(pT_part(i), by(P)(full(dve, "pT", l, i)))
                    ins.then_inc(bank_free[plan[("pT", l, i)][0]], 1)
                dve.wait_ge(S("probs"), 16 * L)
                link(dve.reciprocal(psumv, psumv))
                for tb in range(TB):
                    b = full(dve, "o", l, tb)
                    ins = dve.tensor_tensor(o_at[:, tb].rearrange("p (h d) -> p h d", d=AD),
                                            b[:, :].rearrange("p (h d) -> p h d", d=AD),
                                            wide(psumv[:, 8 * tb:8 * tb + 8], (P, AH, AD)), ALU.mult)
                    ins.then_inc(bank_free[plan[("o", l, tb)][0]], 1)
                dve.wait_ge(S("ho_sq"), L)
                dve.tensor_reduce(hss, flat(lq[0]).rearrange("p (g k) -> p g k", k=HG_K), AX_X, ALU.add
                                  ).then_inc(S("ho_sum"), 1)
                dve.wait_ge(S("ho_rms"), L)
                ho8 = ho.rearrange("p b (h k) -> p (b h) k", k=HG_K)
                ins = dve.tensor_tensor(ho8, full(dve, "ho", l)[:, :].rearrange("p (g k) -> p g k", k=HG_K),
                                        wide(hrr, (P, 8, HG_K)), ALU.mult)
                taken_by(("ho", l), ins)
                dve.tensor_tensor(ho, ho, hgs, ALU.mult).then_inc(S("ho_ready"), 1)
                dve.wait_ge(S("tables"), L)
                for pr in range(4):
                    ct, st = pair(cos_t, pr), pair(sin_t, pr)
                    gr, gi = xr[pr % 2], xi[pr % 2]
                    if pr >= 2:
                        dve.wait_ge(S("states"), 2 * (4 * l + pr - 1))
                    br, bi = by(256)(full(dve, "bu", l, pr, 0)), by(256)(full(dve, "bu", l, pr, 1))
                    dve.tensor_tensor(sv[0], br, ct, ALU.mult)
                    link(dve.tensor_tensor(sv[1], bi, st, ALU.mult))
                    link(dve.tensor_tensor(gr, sv[0], sv[1], ALU.add))
                    taken_by(("bu", l, pr, 1), dve.tensor_tensor(sv[0], bi, ct, ALU.mult))
                    taken_by(("bu", l, pr, 0), dve.tensor_tensor(sv[1], br, st, ALU.mult))
                    link(dve.tensor_tensor(gi, sv[0], sv[1], ALU.subtract))
                    for g in (gr, gi):
                        for i in range(2):
                            j = pr + 4 * i
                            dve.tensor_tensor_scan(g[:, i, :], mag[:, j:j + 1].to_broadcast((P, T)), g[:, i, :], 0.0,
                                                   ALU.mult, ALU.add).then_inc(S("scan"), 1)

                def mix(br, q):
                    g0 = gates[:, 8 * br + 2 * q:8 * br + 2 * q + 2, :]
                    ins = dve.tensor_tensor(g0, g0, by(256)(full(dve, "y", l, br, q)), ALU.mult)
                    taken_by(("y", l, br, q), ins)
                    return g0

                taken(dve, "gate", l, 11)
                for q in range(4):
                    mix(1, q)
                for q in range(4):
                    g2 = mix(2, q)
                    g1 = gates[:, 8 + 2 * q:8 + 2 * q + 2, :]
                    link(dve.tensor_tensor(g1, g1, g2, ALU.add))
                b = full(dve, "ssy", l)
                for m in range(2):
                    ins = dve.scalar_tensor_tensor(ys[:, m, :], uT[:, m, :], scol[:, m:m + 1], b[:, 256 * m:256 * m + 256],
                                                   ALU.mult, ALU.add)
                ins.then_inc(bank_free[plan[("ssy", l)][0]], 1)
                for q in range(4):
                    g0 = mix(0, q)
                    dve.tensor_tensor(g0, g0, gates[:, 8 + 2 * q:8 + 2 * q + 2, :], ALU.add).then_inc(S("mixed"), 1)
                for c in range(4):
                    hs = h_t[:, :, 256 * c:256 * c + 256]
                    ins = dve.scalar_tensor_tensor(hs, hs, ALPHA, by(256)(full(dve, "wo", l, c)), ALU.mult, ALU.add)
                    taken_by(("wo", l, c), ins)
                layer_norm(2 * l)
                if l == 0:
                    for g in range(4):
                        tb, kk = divmod(g, 2)
                        dve.wait_ge(S("xh"), g + 1)
                        part = lambda ap: ap[:, 4 * kk:4 * kk + 4, tb * P:(tb + 1) * P]
                        ins = dve.tensor_tensor(part(xl), by(P)(full(dve, "hT", 0, 0, g)), part(xh).bitcast(F32), ALU.subtract)
                        ins.then_inc(bank_free[plan[("hT", 0, 0, g)][0]], 1)
                    lo(("fg", 0)), lo(("fu", 0))
                    for c in range(CH_FFN):
                        if c + 1 < CH_FFN:
                            lo(("fg", c + 1)), lo(("fu", c + 1))
                        taken(dve, "fg", c)
                        af = flat(a_f[c % 2])
                        ins = dve.tensor_tensor(af, af, full(dve, "fu", c)[:, :], ALU.mult)
                        taken_by(("fu", c), ins)
                        lo(("fd", c))
                        dve.wait_ge(S("ffn_ah"), c + 1)
                        dve.tensor_tensor(a_l[c % 2], a_f[c % 2], a_h[c % 2].bitcast(F32), ALU.subtract
                                          ).then_inc(S("ffn_al"), 1)
                    for tb in range(TB):
                        for hf in range(2):
                            hs = h_t[:, tb, 512 * hf:512 * hf + 512]
                            ins = dve.scalar_tensor_tensor(hs, hs, ALPHA, full(dve, "fd", tb, hf)[:, :], ALU.mult, ALU.add)
                            taken_by(("fd", tb, hf), ins)
                    layer_norm(1)

            for g in range(4):
                taken(dve, "hT", 1, 0, g)
            for tb in range(TB):
                dve.wait_ge(S("ht_h"), tb + 1)
                link(dve.tensor_tensor(ht_l[:, tb, :], h_t[:, tb, :], ht_h[:, tb, :].bitcast(F32), ALU.subtract))
                link(dve.tensor_scalar(h_t[:, tb, :], h_t[:, tb, :], ALPHA, None, ALU.mult))
            lgt, oh1, oh2, tmp, msk, rank, gat = (rt[:, i] for i in range(7))
            r8 = over
            link(dve.tensor_scalar(r8, jrow[:, 0:NE], -1.0, float(NE), ALU.mult, ALU.add))
            r8b = r8.unsqueeze(1).to_broadcast((P, TB, NE))
            b = full(dve, "router")
            ins = dve.tensor_copy(lgt, b[:, 0:TB * NE].rearrange("p (b e) -> p b e", e=NE))
            taken_by(("router",), ins)
            src = lgt
            for oh, m in ((oh1, 0), (oh2, 2)):
                link(dve.tensor_reduce(rs[:, m, :], src, AX_X, ALU.max))
                link(dve.tensor_tensor(tmp, src, wide(rs[:, m, :], (P, TB, NE)), ALU.is_equal))
                link(dve.tensor_tensor(tmp, tmp, r8b, ALU.mult))
                link(dve.tensor_reduce(rs[:, m + 1, :], tmp, AX_X, ALU.max))
                link(dve.tensor_tensor(oh, tmp, wide(rs[:, m + 1, :], (P, TB, NE)), ALU.is_equal))
                if m == 0:
                    link(dve.scalar_tensor_tensor(msk, oh, TAKEN, lgt, ALU.mult, ALU.add))
                    src = msk
            dve.tensor_tensor(rs[:, 5, :], rs[:, 2, :], rs[:, 0, :], ALU.subtract).then_inc(S("top_diff"), 1)
            dve.tensor_tensor(msk, oh1, oh2, ALU.add).then_inc(S("routed"), 1)
            dve.wait_ge(S("top_exp"), 1)
            link(dve.tensor_scalar(rs[:, 7, :], rs[:, 6, :], 1.0, None, ALU.add))
            link(dve.reciprocal(rs[:, 7, :], rs[:, 7, :]))
            link(dve.tensor_tensor(rs[:, 8, :], rs[:, 6, :], rs[:, 7, :], ALU.mult))
            link(dve.tensor_tensor(gat, oh1, wide(rs[:, 7, :], (P, TB, NE)), ALU.mult))
            link(dve.tensor_tensor(tmp, oh2, wide(rs[:, 8, :], (P, TB, NE)), ALU.mult))
            link(dve.tensor_tensor(gat, gat, tmp, ALU.add))
            b = full(dve, "rank")
            link(dve.tensor_scalar(rank, b[:, 0:TB * NE].rearrange("p (b e) -> p b e", e=NE), 1.0, None, ALU.add))
            link(dve.tensor_reduce(cur[:, 3:4], b[:, 2 * NE:3 * NE], AX_X, ALU.max))
            link(dve.tensor_tensor(rank, rank, msk, ALU.mult))
            link(dve.tensor_scalar(rank, rank, -1.0, None, ALU.add))
            dve.tensor_copy(over_i, cur[0:1, 3:4]).then_inc(S("over_ready"), 1)
            taken_by(("rank",), dve.memset(cur[:, 0:1], 0.0))

            SEL_LINKS = 6

            def select(order):
                order(dve.tensor_scalar(rt[:, 7, 0, :], jrow[:, 0:NE], cur[:, 0:1], None, ALU.is_equal))
                e8 = rt[:, 7, 0, :].unsqueeze(1).to_broadcast((P, TB, NE))
                dve.tensor_tensor(rt[:, 8], rank, e8, ALU.mult)
                order(dve.tensor_tensor(rt[:, 9], gat, e8, ALU.mult))
                dve.tensor_reduce(rs[:, 0, :], rt[:, 8], AX_X, ALU.add)
                order(dve.tensor_reduce(rs[:, 1, :], rt[:, 9], AX_X, ALU.add))
                for tb in range(TB):
                    dve.tensor_scalar(sel[:, tb, :], jrow[:, 0:CAP], rs[:, 0, tb:tb + 1], None, ALU.is_equal)
                    order(dve.tensor_scalar(selg[:, tb, :], jrow[:, 0:CAP], rs[:, 0, tb:tb + 1], rs[:, 1, tb:tb + 1],
                                            ALU.is_equal, ALU.mult))
                order(dve.tensor_scalar(cur[:, 0:1], cur[:, 0:1], 1.0, None, ALU.add))
                dve.sem_inc(S("sel"), 1)

            def experts(first):
                with dve.Fori(0, NE) as e:
                    it = e + first
                    order = Link(dve, "dve_loop", start=it * SEL_LINKS)

                    def lo_e(*name):
                        j = moe_at[name]
                        m, (s, _) = (N_SPLIT + j) % SPLIT, moe_slot(j)
                        dve.wait_ge(S("hi_full"), it * N_MOE + (N_SPLIT + j + 1))
                        dve.tensor_tensor(wlo[m], raw[s], whi[m].bitcast(F32), ALU.subtract).then_inc(S("lo_full"), 1)

                    def done_e(ins, *label):
                        ins.then_inc(bank_free[moe_plan[label][0]], 1)

                    for i, dst in ((1, xe_h), (3, xe_l)):
                        done_e(dve.tensor_copy(dst[:, 4:8, :], by(P)(moe_full(dve, it, "xe", i))), "xe", i)
                    for kind in "gu":
                        lo_e(kind, 0, 0), lo_e(kind, 0, 1)
                    for g in range(GR_MOE):
                        if g + 1 < GR_MOE:
                            lo_e("g", g + 1, 0), lo_e("g", g + 1, 1)
                        b, n = moe_bank(("g", g), it)
                        dve.wait_ge(bank_free[b], n + 1)
                        done_e(dve.tensor_tensor(ea[g % 2], ea[g % 2], moe_full(dve, it, "u", g)[:, :], ALU.mult), "u", g)
                        if g + 1 < GR_MOE:
                            lo_e("u", g + 1, 0), lo_e("u", g + 1, 1)
                        dve.wait_ge(S("et_h"), it * GR_MOE + (g + 1))
                        done_e(dve.tensor_tensor(et_l[g % 2], by(P)(moe_full(dve, it, "t", g)),
                                                 et_h[g % 2].bitcast(F32), ALU.subtract), "t", g)
                        lo_e("d", g, 0), lo_e("d", g, 1)
                        if g == 3:
                            select(order)
                    done_e(dve.tensor_copy(y_e[:, 512:1024], moe_full(dve, it, "y", 1)[:, :]), "y", 1)
                    for q in range(4):
                        tb, hf = divmod(q, 2)
                        hs = h_t[:, tb, 512 * hf:512 * hf + 512]
                        done_e(dve.tensor_tensor(hs, hs, moe_full(dve, it, "sc", q)[:, :], ALU.add), "sc", q)
                    assert order.n == SEL_LINKS

            select(link)
            experts(0)
            dve.wait_ge(S("over_ready"), 1)
            with dve.If(dve.value_load(over_i[0:1, 0:1], min_val=0, max_val=T) > CAP):
                again = Link(dve, "dve_again")
                again(dve.tensor_scalar(rank, rank, -float(CAP), None, ALU.add))
                again(dve.memset(cur[:, 0:1], 0.0))
                select(again)
                experts(NE)
            b, n = moe_bank(("sc", 3), NE - 1)
            dve.wait_ge(bank_free[b], n + 1)
            layer_norm(2 * DEPTH - 1)


_INS = ['x', 'w_in', 'ssm_log_dt', 'ssm_lambda_re', 'ssm_lambda_im', 'ssm_b_re', 'ssm_b_im', 'ssm_c_re', 'ssm_c_im',
        'ssm_d', 'ssm_w_glu', 'ssm_b_glu', 'ssm_w_out', 'hgrn_lb_logits', 'hgrn_norm_g', 'hgrn_w_out',
        'attn_q_norm_g', 'attn_kv_norm_g', 'attn_w_uq', 'attn_w_qidx', 'attn_w_ukv', 'attn_w_out', 'w_o',
        'ln_g', 'ln_b', 'ffn_w_gate', 'ffn_w_up', 'ffn_w_down', 'moe_router', 'moe_w_gate', 'moe_w_up', 'moe_w_down']


def kernel(**inputs):
    import numpy as _np
    import concourse.bacc as _bacc
    from concourse import mybir as _mybir
    from concourse.bass_utils import run_bass_kernel_spmd as _run

    nc = _bacc.Bacc("TRN2", target_bir_lowering=False, num_devices=1)
    arrays, args = {}, []
    for name in _INS:
        a = _np.ascontiguousarray(inputs[name])
        arrays[f"in_{name}_dram"] = a
        args.append(nc.dram_tensor(f"in_{name}_dram", a.shape, _mybir.dt.from_np(a.dtype), kind="ExternalInput").ap())
    args.append(nc.dram_tensor("out_0_dram", (1, T, D), F32, kind="ExternalOutput").ap())
    hybrid_kernel(nc, *args)
    r = _run(nc, [arrays], core_ids=[0])
    return r.results[0]["out_0_dram"]
```

```python
import math
from contextlib import ExitStack

import concourse.bass as bass
from concourse import mybir

F32 = mybir.dt.float32
F32R = mybir.dt.float32r
I32 = mybir.dt.int32
U8 = mybir.dt.uint8
ALU = mybir.AluOpType
ACT = mybir.ActivationFunctionType
AX_X = mybir.AxisListType.X

P = 128
T, D, DEPTH = 256, 1024, 2
TB = T // P
KD = D // P
SSM_G, SSM_C, SSM_N = 16, 16, 64
STILES = SSM_G * SSM_N // P
HG_H, HG_K = 4, 64
AH, AD = 8, 64
IH = 4
N_SEL = 64
MASK = -1e30
TAKEN = -3e38
FFN_D, FFN_E, NE = 2816, 3584, 8
ALPHA = (2 * DEPTH) ** 0.25
COL_Q, COL_F, COL_V, COL_G, COL_CQ, COL_KV, COL_GATE = 256, 512, 768, 1024, 1280, 1536, 1732
N_KVI = 128 + 64 + 4
SLOT = 2048
RAW, SPLIT = 6, 3
CAP = 128
MAGIC = 1.5 * 2.0 ** 23
TWO_PI = (6.28125, 0.0019350051879882812, 2 * math.pi - 6.28125 - 0.0019350051879882812)
CH_FFN = FFN_D // 256
GR_MOE = FFN_E // 512


def psum_plan():
    order = []

    def use(bank, *label):
        order.append((label, bank))

    for g in range(4):
        use(g, "xT", g)
    for l in range(DEPTH):
        for b, n in enumerate(("cq", "kvi", "u", "hq", "hf", "hv", "hg")):
            use(b, n, l)
        use(7, "bt", l), use(2, "cct", l)
        use(3, "cqT", l), use(0, "kviT", l)
        use(1, "gate", l, 0)
        use(2, "q", l, 0), use(3, "q", l, 1), use(4, "qi", l), use(5, "k", l, 0), use(6, "k", l, 1)
        use(7, "v", l, 0), use(0, "v", l, 1)
        use(1, "gate", l, 1)
        use(2, "idx", l, 0), use(3, "idx", l, 1), use(4, "idx", l, 2), use(7, "idx", l, 3)
        use(5, "gate", l, 2), use(6, "gate", l, 3)
        use(2, "lg", l, 0), use(3, "lg", l, 1)
        use(4, "lg", l, 2), use(7, "lg", l, 3), use(0, "lg", l, 4), use(1, "lg", l, 5)
        use(5, "gate", l, 4), use(6, "gate", l, 5)
        n = 0
        for lv in range(8):
            for odd in range(2):
                use((5, 6)[n % 2], "lev", l, lv, odd)
                n += 1
            if lv in (2, 4, 6):
                use(2, "gate", l, 5 + lv // 2)
        use(5, "lev", l, 8, 0), use(6, "lev", l, 8, 1)
        for i in range(6):
            use((7, 0)[i % 2], "pT", l, i)
            if i == 1:
                use(3, "o", l, 0)
        use(4, "o", l, 1)
        use(6, "ho", l)
        for pr in range(4):
            use((0, 2)[pr % 2], "bu", l, pr, 0), use((1, 3)[pr % 2], "bu", l, pr, 1)
            if pr == 0:
                use(5, "gate", l, 9)
            if pr == 1:
                use(7, "oT", l, 0), use(5, "oT", l, 1)
                use(6, "gate", l, 10)
            if pr == 2:
                use(5, "hoT", l)
                use(7, "gate", l, 11)
        use(4, "ssy", l)
        for q in range(4):
            use((5, 6, 0, 1)[q], "y", l, 1, q)
        for q in range(4):
            use((5, 6, 0, 1)[q], "y", l, 2, q)
        use(7, "glu", l)
        for q in range(4):
            use((5, 6, 0, 1)[q], "y", l, 0, q)
        for c in range(4):
            use(c, "wo", l, c)
        for g in range(4):
            use(4 + g, "hT", l, 0, g)
        if l == 0:
            for tb in range(TB):
                for hf in range(2):
                    use(4 + 2 * tb + hf, "fd", tb, hf)
            for c in range(CH_FFN):
                use(c % 2, "fg", c), use(2 + c % 2, "fu", c)
            for g in range(4):
                use(g, "hT", l, 1, g)
        else:
            use(0, "router"), use(1, "rank")
    seen, plan = [0] * 8, {}
    for label, bank in order:
        assert label not in plan, label
        plan[label] = (bank, seen[bank])
        seen[bank] += 1
    return plan, seen


def hybrid_kernel(nc, x, w_in, log_dt, lam_re, lam_im, b_re, b_im, c_re, c_im, ssm_d, w_glu, b_glu, ssm_w_out,
                  lb_logits, hg_norm_g, hg_w_out, q_norm_g, kv_norm_g, w_uq, w_qidx, w_ukv, att_w_out, w_o,
                  ln_g, ln_b, ffn_gate, ffn_up, ffn_down, router, moe_gate, moe_up, moe_down, out):
    plan, bank_uses = psum_plan()

    jobs = []

    def tiles(src, r0, k, c0, n):
        return src[r0:r0 + k * P, c0:c0 + n].rearrange("(k p) n -> p k n", p=P)

    for l in range(DEPTH):
        for name, c0, n in (("cq", COL_CQ, 256), ("kvi", COL_KV, N_KVI), ("u", 0, 256), ("hq", COL_Q, 256),
                            ("hf", COL_F, 256), ("hv", COL_V, 256), ("hg", COL_G, 256)):
            jobs.append(((name, l), [(0, (KD, n), tiles(w_in[l], 0, KD, c0, n))]))

        def gate_job(c):
            jobs.append((("gate", l, c), [(0, (KD, 256), tiles(w_in[l], 0, KD, COL_GATE + 256 * c, 256))]))

        gate_job(0)
        jobs.append((("uq", l), [(0, (2, 512), tiles(w_uq[l], 0, 2, 0, 512)),
                                 (1024, (2, 256), tiles(w_qidx[l], 0, 2, 0, 256))]))
        jobs.append((("ukv", l), [(0, (1, 1024), tiles(w_ukv[l], 0, 1, 0, 1024))]))
        for c in range(1, 12):
            gate_job(c)
        jobs.append((("wout", l, 1), [(0, (2, D), tiles(hg_w_out[l], 0, 2, 0, D))]))
        for k in range(2):
            jobs.append((("wout", l, 2, k), [(0, (2, D), tiles(att_w_out[l], 2 * k * P, 2, 0, D))]))
        jobs.append((("glu", l), [(0, (2, 256), tiles(w_glu[l], 0, 2, 0, 256))]))
        jobs.append((("wout", l, 0), [(0, (2, D), tiles(ssm_w_out[l], 0, 2, 0, D))]))
        for c in range(4):
            jobs.append((("wo", l, c), [(0, (KD, 256), tiles(w_o[l], 0, KD, 256 * c, 256))]))
        if l == 0:
            for c in range(CH_FFN + 1):
                if c < CH_FFN:
                    jobs.append((("fg", c), [(0, (KD, 256), tiles(ffn_gate[0], 0, KD, 256 * c, 256))]))
                    jobs.append((("fu", c), [(0, (KD, 256), tiles(ffn_up[0], 0, KD, 256 * c, 256))]))
                if c > 0:
                    jobs.append((("fd", c - 1), [(0, (2, D), tiles(ffn_down[0], 256 * (c - 1), 2, 0, D))]))
    job_at = {name: n for n, (name, _) in enumerate(jobs)}
    full_value, filled = [], [0] * RAW
    for n, (_, parts) in enumerate(jobs):
        filled[n % RAW] += 16 * len(parts)
        full_value.append(filled[n % RAW])
    N_JOBS = len(jobs)
    split_names = [n for n, _ in jobs if n[0] in ("fg", "fu", "fd")]
    split_at = {name: m for m, name in enumerate(split_names)}
    N_SPLIT = len(split_names)

    moe_jobs = []
    for g in range(GR_MOE + 1):
        if g < GR_MOE:
            moe_jobs += [("g", g, 0), ("g", g, 1), ("u", g, 0), ("u", g, 1)]
        if g > 0:
            moe_jobs += [("d", g - 1, 0), ("d", g - 1, 1)]
    N_MOE = len(moe_jobs)
    moe_at = {name: j for j, name in enumerate(moe_jobs)}
    assert N_MOE % RAW == 0 and N_MOE % SPLIT == 0 and N_SPLIT % SPLIT == 0

    ctx = ExitStack()
    with ctx:
        arena = [nc.sbuf_base + (-nc.sbuf_base) % 32]

        def place(name, shape, dt, at):
            return nc.alloc_sbuf_tensor_at(name, shape, dt, offset=at).ap()

        def nbytes(shape, dt):
            n = 1 if dt == U8 else 4
            for s in shape[1:]:
                n *= s
            return n + (-n) % 32

        def sb(name, shape, dt=F32):
            at = arena[0]
            arena[0] += nbytes(shape, dt)
            return place(name, shape, dt, at)

        sems = {}

        def S(name):
            if name not in sems:
                sems[name] = ctx.enter_context(nc.semaphore(name))
            return sems[name]

        bank = [ctx.enter_context(nc.psum_tensor(f"bank{b}", [P, 512], F32))[:, :] for b in range(8)]
        raw_full = [S(f"raw_full{i}") for i in range(RAW)]
        bank_full = [S(f"bank_full{i}") for i in range(8)]
        bank_free = [S(f"bank_free{i}") for i in range(8)]

        raw = [sb(f"raw{i}", [P, SLOT]) for i in range(RAW)]
        h_t = sb("h_t", [P, TB, D])
        cos_t = sb("cos_t", [P, STILES, T])
        sin_t = sb("sin_t", [P, STILES, T])
        lng = sb("lng", [P, 2, D])
        ident = sb("ident", [P, P])
        negd = sb("negd", [P, 3 * P])
        lev_mask = sb("lev_mask", [P, 8, P], U8)
        tri = sb("tri", [P, P])
        ones = sb("ones", [P, P])
        jrow = sb("jrow", [P, P])
        pow_m = sb("pow_m", [P, 2])
        par = sb("par", [P, 2])
        par_i = sb("par_i", [P, 2], I32)
        ip = sb("ip", [P, P], I32)
        jf = sb("jf", [P, P], I32)
        lam = sb("lam", [P, 3, STILES])
        mag = sb("mag", [P, STILES])
        sc = sb("sc", [P, 16, STILES])
        wpow = sb("wpow", [P, 2, 8, STILES])
        bbT = sb("bbT", [P, 2, 2, P])
        ccT = sb("ccT", [P, 2, 2, P])
        scol = sb("scol", [P, 11])
        lbl = sb("lbl", [P, 2, 2])
        hgn = sb("hgn", [P, HG_K])
        stat = sb("stat", [P, 96])
        wrt = sb("wrt", [P, KD, NE])
        small_end = arena[0]

        hT = sb("hT", [P, KD, T])
        gates = sb("gates", [P, 24, T])
        cqs = sb("cqs", [P, TB, 512])
        o_at = place("o_at", [P, TB, 512], F32, arena[0] - 4096)
        qT = sb("qT", [P, 4, T])
        oT = place("oT", [P, 4, T], F32, arena[0] - 4096)
        cT = sb("cT", [P, 4, T])
        qiT = sb("qiT", [P, 2, T])
        kT = sb("kT", [P, 4, T])
        v_at = sb("v_at", [P, TB, 512])
        widx = sb("widx", [P, TB, IH])
        score = sb("score", [P, 3 * P])
        work = sb("work", [P, 3 * P])
        top8 = sb("top8", [P, 8])
        ssm_base = arena[0]
        prob = sb("prob", [P, 8 * 384])
        pT = sb("pT", [P, 2, 8, P])
        relu_s = place("relu_s", [P, 4 * 384], F32, ssm_base)
        xr = [place(f"xr{i}", [P, 2, T], F32, ssm_base + 2048 * i) for i in range(2)]
        xi = [place(f"xi{i}", [P, 2, T], F32, ssm_base + 4096 + 2048 * i) for i in range(2)]
        sv = [place(f"sv{i}", [P, 2, T], F32, ssm_base + 8192 + 2048 * i) for i in range(2)]
        hre = place("hre", [P, 2, T], F32, ssm_base + 12288)
        him = place("him", [P, 2, T], F32, ssm_base + 14336)
        sp_ = [place(f"sp{i}", [P, 2, T], F32, ssm_base + 16384 + 2048 * i) for i in range(2)]
        uT = sb("uT", [P, 2, T])
        tmp_at = arena[0]
        ys = sb("ys", [P, 2, T])
        yg = sb("yg", [P, 2, T])
        ysig = sb("ysig", [P, 2, T])
        hq = sb("hq", [P, 2, T])
        hk = sb("hk", [P, 2, T])
        hP = sb("hP", [P, 2, T])
        hR = sb("hR", [P, 2, T])
        lq = [sb(f"lq{i}", [P, 2, T]) for i in range(2)]
        lk = [sb(f"lk{i}", [P, 2, T]) for i in range(2)]
        h_att = sb("h_att", [P, 3, 4, P])
        hv = sb("hv", [P, TB, 256])
        hgs = sb("hgs", [P, TB, 256])
        ho = sb("ho", [P, TB, 256])
        hoT = sb("hoT", [P, 2, T])
        b_raw = sb("b_raw", [P, 2, STILES, SSM_C])
        mix_end = arena[0]

        arena[0] = small_end
        split_mem = [sb(f"split{i}", [P, SLOT], F32R) for i in range(2 * SPLIT)]
        whi = [split_mem[i] for i in (0, 1, 2)]
        wlo = [split_mem[i] for i in (4, 3, 5)]
        shared_end = arena[0]
        xh = sb("xh", [P, KD, T], F32R)
        xl = sb("xl", [P, KD, T], F32R)
        a_f = [sb(f"a_f{i}", [P, 2, T]) for i in range(2)]
        a_h = [sb(f"a_h{i}", [P, 2, T], F32R) for i in range(2)]
        a_l = [sb(f"a_l{i}", [P, 2, T], F32R) for i in range(2)]
        ffn_end = arena[0]
        arena[0] = shared_end
        ht_h = sb("ht_h", [P, TB, D], F32R)
        ht_l = sb("ht_l", [P, TB, D], F32R)
        xe_h = sb("xe_h", [P, KD, CAP], F32R)
        xe_l = sb("xe_l", [P, KD, CAP], F32R)
        ea = [sb(f"ea{i}", [P, 512]) for i in range(2)]
        et_h = [sb(f"et_h{i}", [P, 4, CAP], F32R) for i in range(2)]
        et_l = [sb(f"et_l{i}", [P, 4, CAP], F32R) for i in range(2)]
        y_e = sb("y_e", [P, D])
        sel = sb("sel", [P, TB, CAP], F32R)
        selg = sb("selg", [P, TB, CAP])
        selT = sb("selT", [P, TB, CAP])
        hTr = sb("hTr", [P, KD, T])
        rt = sb("rt", [P, 12, TB, NE])
        rs = sb("rs", [P, 10, TB])
        cur = sb("cur", [P, 4])
        over = sb("over", [P, 8])
        over_i = sb("over_i", [1, 1], I32)
        moe_end = arena[0]
        tab_tmp = [place("tab_tmp0", [P, STILES, P], F32, tmp_at), place("tab_tmp1", [P, STILES, P], F32, ffn_end)]
        c_raw = place("c_raw", [P, 2, 2, SSM_N], F32, ssm_base)
        c_exp = place("c_exp", [P, 2, 2, P], F32, ssm_base + 1024)
        b_exp = place("b_exp", [P, 2, STILES, 32], F32, ssm_base + 1024 + 2048)
        b_tmp = place("b_tmp", [P, 2, STILES, SSM_C], F32, ssm_base + 5120)
        assert max(mix_end, ffn_end, moe_end) <= nc.sbuf_usable_end

        MS, MEAN, RMS = stat[:, 0:4], stat[:, 4:8], stat[:, 8:12]
        bn6 = stat[:, 12:36].rearrange("p (b h s) -> p b h s", b=TB, h=2)
        mv = stat[:, 36:40].rearrange("p (b s) -> p b s", b=TB)
        rstd, veps = stat[:, 40:42], stat[:, 42:44]
        nmax, psumv = stat[:, 44:60], stat[:, 60:76]
        hss, hrr = stat[:, 76:84], stat[:, 84:92]
        prob0 = prob[:, 0:1024].rearrange("p (h s) -> p h s", h=AH)
        prob1 = prob[:, 1024:3072].rearrange("p (h s) -> p h s", h=AH)
        probs = [prob0, prob1]
        LAYER = lambda l: l + 1

        def wide(ap, shape):
            return ap.unsqueeze(len(ap.shape)).to_broadcast(shape)

        def full(eng, *label):
            b, n = plan[label]
            eng.wait_ge(bank_full[b], n + 1)
            return bank[b]

        def taken(eng, *label):
            b, n = plan[label]
            eng.wait_ge(bank_free[b], n + 1)

        def pT_part(i):
            hg, kb = i % 2, (0, 1, 0)[i // 2]
            return pT[:, kb, 4 * hg:4 * hg + 4, :]

        def pair(ap, pr):
            return ap.rearrange("p (m j) t -> p j m t", m=2)[:, pr]

        def by(n):
            return lambda b: b[:, :].rearrange("p (a n) -> p a n", n=n)

        class Link:

            def __init__(self, eng, name, start=0):
                self.eng, self.sem, self.n, self.start = eng, S(name), 0, start

            def __call__(self, ins):
                self.n += 1
                ins.then_inc(self.sem, 1)
                self.eng.wait_ge(self.sem, self.start + self.n)

        gather_order = [(("xe", 0), 6), (("xe", 1), 1), (("xe", 2), 3), (("xe", 3), 2)]

        def expert_order(last):
            order = [(("g", 0), 0), (("u", 0), 2)]
            for g in range(GR_MOE):
                if g + 1 < GR_MOE:
                    order.append((("g", g + 1), (g + 1) % 2))
                if g == 0:
                    order.append((("selT",), 6))
                order.append((("t", g), 7 if g % 2 == 0 else 6))
                if g + 1 < GR_MOE:
                    order.append((("u", g + 1), 2 + (g + 1) % 2))
                if g == 0:
                    order += [(("y", 0), 4), (("y", 1), 5)]
            if not last:
                order += gather_order
            return order + [(("sc", q), (7, 6, 3, 1)[q]) for q in range(4)]

        def numbered(order):
            uses, plan_ = [0] * 8, {}
            for label, b in order:
                plan_[label] = (b, uses[b])
                uses[b] += 1
            return plan_, uses

        gather_plan, gather_uses = numbered(gather_order)
        body_plan, body_uses = numbered(expert_order(False))
        last_plan, last_uses = numbered(expert_order(True))

        class Expert:

            def __init__(self, second, e, last=False):
                self.e, self.last, self.start = e, last, e is None
                self.it = second * NE + (0 if e is None else e)
                self.second = second
                self.plan = gather_plan if e is None else last_plan if last else body_plan

            def at(self, *label):
                b, k = self.plan[label]
                n = bank_uses[b] + k + self.second * (gather_uses[b] + (NE - 1) * body_uses[b] + last_uses[b])
                if not self.start:
                    n = self.e * body_uses[b] + (n + gather_uses[b])
                return b, n

            def full(self, eng, *label):
                b, n = self.at(*label)
                eng.wait_ge(bank_full[b], n + 1)
                return bank[b]

            def taken(self, eng, *label):
                b, n = self.at(*label)
                eng.wait_ge(bank_free[b], n + 1)

        def run_pass(eng, second, start, body):
            start(Expert(second, None))
            with nc.Fori(0, NE - 1, engines=[eng.engine], hint_back_edge=True) as e:
                body(Expert(second, e))
            body(Expert(second, NE - 1, last=True))

        def moe_slot(j):
            s = (N_JOBS + j) % RAW
            return s, j // RAW

        last_use = {"uq": ("qi",), "ukv": ("v", 1), "glu": ("glu",)}

        def released(eng, n):
            name = jobs[n][0]
            if name in split_at:
                eng.wait_ge(S("lo_full"), split_at[name] + 1)
                return
            kind, l = name[:2]
            label = name
            if kind == "wout":
                label = ("y", l, name[2], 3)
            elif kind == "wo":
                label = ("wo", l, name[2] | 1)
            elif kind in last_use:
                label = (last_use[kind][0], l) + last_use[kind][1:]
            full(eng, *label)

        PER_SLOT = N_MOE // RAW
        block = ctx.enter_context(nc.Block())

        @block.sync
        def _(sp):
            for tb in range(TB):
                sp.dma_start(h_t[:, tb, :], x[0, tb * P:(tb + 1) * P, :]).then_inc(S("x_in"), 16)
            for n, (name, parts) in enumerate(jobs):
                if n >= RAW:
                    released(sp, n - RAW)
                for at, (k, m), src in parts:
                    dst = raw[n % RAW][:, at:at + k * m].rearrange("p (k n) -> p k n", k=k)
                    sp.dma_start(dst, src).then_inc(raw_full[n % RAW], 16)

            def load(e, it, j, ahead=0):
                kind, g, hf = moe_jobs[j]
                s, turn = moe_slot(j)
                if it is not None:
                    sp.wait_ge(S("lo_full"), it * N_MOE + (N_SPLIT + j + ahead * N_MOE - RAW + 1))
                if kind == "d":
                    src = moe_down[0, ahead:][bass.ds(e, 1)][:, 512 * g + 256 * hf:512 * g + 256 * hf + 256, :]
                else:
                    w = moe_gate if kind == "g" else moe_up
                    src = w[0, ahead:][bass.ds(e, 1)][:, 512 * hf:512 * hf + 512, 512 * g:512 * g + 512]
                src = src.rearrange("e (k p) n -> p (e k) n", p=P)
                dst = raw[s][:, :].rearrange("p (k n) -> p k n", k=src.shape[1])
                sp.dma_start(dst, src).then_inc(raw_full[s], 16)

            FIRST = moe_at["d", 0, 0]
            assert FIRST >= RAW

            def experts(second):
                with nc.Fori(0, NE - 1, engines=[sp.engine], hint_back_edge=True) as e:
                    it = e + second * NE
                    for j in range(FIRST, N_MOE):
                        load(e, it, j)
                    for j in range(FIRST):
                        load(e, it, j, ahead=1)
                for j in range(FIRST, N_MOE):
                    load(NE - 1, (second + 1) * NE - 1, j)

            for j in range(FIRST):
                if j < RAW:
                    released(sp, N_JOBS - RAW + j)
                load(0, None if j < RAW else 0, j)
            experts(0)
            sp.wait_ge(S("over_ready"), 1)
            with sp.If(sp.value_load(over_i[0:1, 0:1], min_val=0, max_val=T) > CAP):
                for j in range(FIRST):
                    load(0, NE, j)
                experts(1)
            for tb in range(TB):
                sp.wait_ge(S("h_ready"), 2 * (2 * DEPTH - 1) + tb + 1)
                sp.dma_start(out[0, tb * P:(tb + 1) * P, :], h_t[:, tb, :]).then_inc(S("stored"), 16)
            sp.wait_ge(S("stored"), 32)

        @block.gpsimd
        def _(pool):
            link = Link(pool, "pool_link")
            pool.memset(ident, 0.0).then_inc(S("c0"), 1)
            pool.memset(ones, 1.0).then_inc(S("c0"), 1)
            pool.memset(tri, 1.0).then_inc(S("c0"), 1)
            pool.memset(pow_m[:, 0:1], -0.5).then_inc(S("c0"), 1)
            pool.memset(pow_m[:, 1:2], -1.0).then_inc(S("c0"), 1)
            pool.iota(ip, pattern=[[0, P]], base=0, channel_multiplier=1).then_inc(S("c0"), 1)
            pool.iota(jf, pattern=[[1, P]], base=0, channel_multiplier=0).then_inc(S("c0"), 1)
            pool.iota(jrow, pattern=[[1, P]], base=0, channel_multiplier=0,
                      allow_small_or_imprecise_dtypes=True).then_inc(S("c0"), 1)
            pool.iota(negd[:, 0:P], pattern=[[1, P]], base=0, channel_multiplier=-1,
                      allow_small_or_imprecise_dtypes=True).then_inc(S("c0"), 1)
            pool.iota(negd[:, P:3 * P], pattern=[[1, T]], base=-P, channel_multiplier=-1,
                      allow_small_or_imprecise_dtypes=True).then_inc(S("c0"), 1)
            pool.wait_ge(S("c0"), 10)
            pool.affine_select(out=ident, in_=ident, compare_op=ALU.not_equal, fill=1.0, base=0,
                               pattern=[[-1, P]], channel_multiplier=1).then_inc(S("consts"), 1)
            pool.affine_select(out=tri, in_=tri, compare_op=ALU.is_gt, fill=0.0, base=0,
                               pattern=[[1, P]], channel_multiplier=-1).then_inc(S("consts"), 1)
            for part in (negd[:, 0:P], negd[:, 2 * P:3 * P]):
                pool.affine_select(out=part, in_=part, compare_op=ALU.is_ge, fill=MASK, base=0,
                                   pattern=[[-1, P]], channel_multiplier=1).then_inc(S("consts"), 1)

            def tables(l):
                pool.dma_start(lam[:, 0, :], lam_re[l].rearrange("(j g) p -> (g p) j", g=2),
                               allow_slow_non_contiguous=True).then_inc(S("lam_in"), 16)
                pool.dma_start(lam[:, 1, :], lam_im[l].rearrange("(j g) p -> (g p) j", g=2),
                               allow_slow_non_contiguous=True).then_inc(S("lam_in"), 16)
                for g in range(2):
                    pool.dma_start(lam[64 * g:64 * g + 64, 2, :],
                                   log_dt[l:l + 1].rearrange("o (j g) -> o g j", g=2)[:, g, :].to_broadcast((64, STILES)),
                               allow_slow_non_contiguous=True).then_inc(S("lam_in"), 16)
                pool.wait_ge(S("dt"), LAYER(l))
                pool.tensor_tensor(sc[:, 1, :], lam[:, 0, :], sc[:, 0, :], ALU.mult).then_inc(S("expo"), 1)
                link(pool.tensor_tensor(sc[:, 2, :], lam[:, 1, :], sc[:, 0, :], ALU.mult))
                link(pool.tensor_scalar(sc[:, 3, :], sc[:, 2, :], 1 / (2 * math.pi), MAGIC, ALU.mult, ALU.add))
                link(pool.tensor_scalar(sc[:, 3, :], sc[:, 3, :], -MAGIC, 1.0, ALU.add, ALU.mult))
                for c in TWO_PI:
                    link(pool.tensor_scalar(sc[:, 4, :], sc[:, 3, :], -c, 0.0, ALU.mult, ALU.add))
                    link(pool.tensor_tensor(sc[:, 2, :], sc[:, 4, :], sc[:, 2, :], ALU.add))
                link(pool.tensor_scalar(sc[:, 4, :], sc[:, 2, :], 3.1415925, -3.1415925, ALU.min, ALU.max))
                pool.tensor_scalar(sc[:, 5, :], sc[:, 4, :], 0.5, 0.0, ALU.mult, ALU.add).then_inc(S("angle"), 1)
                pool.wait_ge(S("sines"), 2 * LAYER(l))
                link(pool.tensor_tensor(sc[:, 8, :], sc[:, 7, :], sc[:, 7, :], ALU.mult))
                link(pool.tensor_scalar(sc[:, 8, :], sc[:, 8, :], -2.0, 1.0, ALU.mult, ALU.add))
                pool.wait_ge(S("mag"), LAYER(l))
                link(pool.tensor_tensor(sc[:, 9, :], mag, sc[:, 8, :], ALU.mult))
                link(pool.tensor_tensor(sc[:, 10, :], mag, sc[:, 6, :], ALU.mult))
                link(pool.tensor_scalar(sc[:, 11, :], sc[:, 9, :], -1.0, 1.0, ALU.add, ALU.mult))
                link(pool.tensor_tensor(sc[:, 12, :], lam[:, 0, :], lam[:, 0, :], ALU.mult))
                link(pool.tensor_tensor(sc[:, 13, :], lam[:, 1, :], lam[:, 1, :], ALU.mult))
                link(pool.tensor_tensor(sc[:, 12, :], sc[:, 12, :], sc[:, 13, :], ALU.add))
                link(pool.tensor_tensor(sc[:, 12, :], sc[:, 12, :], pow_m[:, 1:2].to_broadcast((P, STILES)), ALU.pow))
                link(pool.tensor_tensor(sc[:, 13, :], sc[:, 11, :], lam[:, 0, :], ALU.mult))
                link(pool.tensor_tensor(sc[:, 14, :], sc[:, 10, :], lam[:, 1, :], ALU.mult))
                link(pool.tensor_tensor(sc[:, 13, :], sc[:, 13, :], sc[:, 14, :], ALU.add))
                link(pool.tensor_tensor(sc[:, 13, :], sc[:, 13, :], sc[:, 12, :], ALU.mult))
                link(pool.tensor_tensor(sc[:, 14, :], sc[:, 10, :], lam[:, 0, :], ALU.mult))
                link(pool.tensor_tensor(sc[:, 15, :], sc[:, 11, :], lam[:, 1, :], ALU.mult))
                link(pool.tensor_tensor(sc[:, 14, :], sc[:, 14, :], sc[:, 15, :], ALU.subtract))
                link(pool.tensor_tensor(sc[:, 14, :], sc[:, 14, :], sc[:, 12, :], ALU.mult))

            def rotations(l):
                pool.memset(cos_t[:, :, 0:1], 1.0)
                pool.memset(sin_t[:, :, 0:1], 0.0)
                link(pool.tensor_copy(wpow[:, 0, 0, :], sc[:, 8, :]))
                link(pool.tensor_copy(wpow[:, 1, 0, :], sc[:, 6, :]))
                for i in range(8):
                    n = 1 << i
                    wc = wide(wpow[:, 0, i, :], (P, STILES, n))
                    ws = wide(wpow[:, 1, i, :], (P, STILES, n))
                    c0, s0, c1, s1 = cos_t[:, :, 0:n], sin_t[:, :, 0:n], cos_t[:, :, n:2 * n], sin_t[:, :, n:2 * n]
                    t0 = tab_tmp[l][:, :, 0:n]
                    pool.tensor_tensor(c1, c0, wc, ALU.mult)
                    link(pool.tensor_tensor(t0, s0, ws, ALU.mult))
                    link(pool.tensor_tensor(c1, c1, t0, ALU.subtract))
                    pool.tensor_tensor(s1, c0, ws, ALU.mult)
                    link(pool.tensor_tensor(t0, s0, wc, ALU.mult))
                    link(pool.tensor_tensor(s1, s1, t0, ALU.add))
                    if i < 7:
                        link(pool.tensor_tensor(sc[:, 8, :], wpow[:, 1, i, :], wpow[:, 1, i, :], ALU.mult))
                        link(pool.tensor_tensor(wpow[:, 0, i + 1, :], wpow[:, 0, i, :], wpow[:, 0, i, :], ALU.mult))
                        link(pool.tensor_tensor(wpow[:, 0, i + 1, :], wpow[:, 0, i + 1, :], sc[:, 8, :], ALU.subtract))
                        link(pool.tensor_tensor(sc[:, 8, :], wpow[:, 0, i, :], wpow[:, 1, i, :], ALU.mult))
                        link(pool.tensor_scalar(wpow[:, 1, i + 1, :], sc[:, 8, :], 2.0, 0.0, ALU.mult, ALU.add))
                pool.sem_inc(S("tables"), 1)

            def load_norm(n):
                l, j = divmod(n, 2)
                if n > 0:
                    pool.wait_ge(S("h_ready"), 2 * n)
                pool.dma_start(lng[:, 0, :], ln_g[l, j:j + 1, :].to_broadcast((P, D))).then_inc(S("norm_in"), 16)
                pool.dma_start(lng[:, 1, :], ln_b[l, j:j + 1, :].to_broadcast((P, D))).then_inc(S("norm_in"), 16)

            def rsqrt(dst, src, tmp, scale, eps):
                link(pool.tensor_scalar(tmp, src, scale, eps, ALU.mult, ALU.add))
                return pool.tensor_tensor(dst, tmp, pow_m[:, 0:1].to_broadcast(tuple(dst.shape)), ALU.pow)

            def norm(n):
                for tb in range(TB):
                    pool.wait_ge(S("norm_var"), TB * n + tb + 1)
                    rsqrt(rstd[:, tb:tb + 1], mv[:, tb, 1:2], veps[:, tb:tb + 1], 1.0, 1e-5).then_inc(S("norm_rstd"), 1)

            tables(0)
            for l in range(DEPTH):
                L = LAYER(l)
                if l > 0:
                    pool.wait_ge(S("h_ready"), 4 * l)
                for ri, src in enumerate((b_re, b_im)):
                    pool.dma_start(b_raw[:, ri], src[l].rearrange("(j g) p c -> (g p) j c", g=2)).then_inc(S("bc_in"), 16)
                for ri, src in enumerate((c_re, c_im)):
                    pool.dma_start(c_raw[:, ri], src[l].rearrange("(m g) c p -> (g c) m p", m=2)).then_inc(S("bc_in"), 16)
                cols = [(0, ssm_d[l]), (2, b_glu[l]), (4, q_norm_g[l])]
                for c, src in cols:
                    pool.dma_start(scol[:, c:c + 2], src.rearrange("(m p) -> p m", p=P),
                               allow_slow_non_contiguous=True).then_inc(S("col_in"), 16)
                pool.dma_start(scol[:, 6:7], kv_norm_g[l].rearrange("(m p) -> p m", p=P),
                               allow_slow_non_contiguous=True).then_inc(S("col_in"), 16)
                for i in range(2):
                    pool.dma_start(lbl[:, i, :], lb_logits[i].rearrange("(m p) -> p m", p=P),
                               allow_slow_non_contiguous=True).then_inc(S("col_in"), 16)
                pool.dma_start(hgn, hg_norm_g[l:l + 1, :].to_broadcast((P, HG_K))).then_inc(S("col_in"), 16)
                load_norm(2 * l)
                if l == DEPTH - 1:
                    pool.dma_start(wrt, router[0].rearrange("(k p) e -> p k e", p=P)).then_inc(S("router_in"), 16)
                pool.memset(b_exp, 0.0)
                pool.memset(h_att, 0.0).then_inc(S("h_att_zero"), 1)
                for b in range(2):
                    pool.memset(lq[b], 0.0).then_inc(S("lev_zero"), 1)
                    link(pool.memset(lk[b], 0.0))
                pool.wait_ge(S("par"), 1)
                pool.wait_ge(S("bc_in"), 64 * L)
                cre = wide(sc[:, 13, :], (P, STILES, SSM_C))
                cim = wide(sc[:, 14, :], (P, STILES, SSM_C))
                for ri, (w0, w1, op) in enumerate(((cre, cim, ALU.subtract), (cim, cre, ALU.add))):
                    pool.tensor_tensor(b_tmp[:, 0], b_raw[:, 0], w0, ALU.mult)
                    link(pool.tensor_tensor(b_tmp[:, 1], b_raw[:, 1], w1, ALU.mult))
                    for g in range(2):
                        r = slice(64 * g, 64 * g + 64)
                        ins = pool.tensor_tensor(b_exp[r, ri, :, SSM_C * g:SSM_C * (g + 1)], b_tmp[r, 0], b_tmp[r, 1], op)
                        if g == 0 or ri == 0:
                            link(ins)
                        else:
                            ins.then_inc(S("b_exp_ready"), 1)
                pool.wait_ge(S("b_exp_ready"), L)
                for ri in range(2):
                    for g in range(2):
                        pool.tensor_scalar(c_exp[:, ri, :, 64 * g:64 * g + 64], c_raw[:, ri], par[:, g:g + 1], 1.0,
                                           ALU.mult, ALU.mult).then_inc(S("c_exp"), 1)

                pool.wait_ge(S("squares"), 4 * L)
                pool.tensor_scalar(MEAN[:, 0:2], MS[:, 0:2], 1.0 / 256, 1e-6, ALU.mult, ALU.add)
                link(pool.tensor_scalar(MEAN[:, 2:4], MS[:, 2:4], 1.0 / 128, 1e-6, ALU.mult, ALU.add))
                pool.tensor_tensor(RMS, MEAN, pow_m[:, 0:1].to_broadcast((P, 4)), ALU.pow).then_inc(S("rms"), 1)
                if l == 0:
                    rotations(0)
                pool.wait_ge(S("ho_sum"), L)
                rsqrt(hrr, hss, hss, 1.0 / HG_K, 1e-6).then_inc(S("ho_rms"), 1)
                for pr in range(4):
                    ct, st = pair(cos_t, pr), pair(sin_t, pr)
                    gr, gi = xr[pr % 2], xi[pr % 2]
                    pool.wait_ge(S("scan"), 4 * (4 * l + pr + 1))
                    if pr > 0:
                        pool.wait_ge(S("states_used"), 3 * l + pr)
                    pool.tensor_tensor(hre, gr, ct, ALU.mult)
                    link(pool.tensor_tensor(sp_[0], gi, st, ALU.mult))
                    pool.tensor_tensor(him, gr, st, ALU.mult)
                    pool.tensor_tensor(sp_[1], gi, ct, ALU.mult).then_inc(S("scan_used"), 1)
                    pool.tensor_tensor(hre, hre, sp_[0], ALU.subtract).then_inc(S("states"), 1)
                    pool.wait_ge(S("scan_used"), 4 * l + pr + 1)
                    pool.tensor_tensor(him, him, sp_[1], ALU.add).then_inc(S("states"), 1)
                taken(pool, "ssy", l)
                link(pool.tensor_tensor(yg, ys, ys, ALU.mult))
                link(pool.tensor_scalar(yg, yg, 0.044715, 1.0, ALU.mult, ALU.add))
                pool.tensor_tensor(yg, yg, ys, ALU.mult).then_inc(S("gelu_in"), 1)
                pool.wait_ge(S("gelu_sig"), L)
                pool.tensor_tensor(yg, ys, ysig, ALU.mult).then_inc(S("gelu"), 1)
                taken(pool, "glu", l)
                pool.wait_ge(S("gelu"), L)
                pool.tensor_tensor(ys, yg, ysig, ALU.mult).then_inc(S("ssm_out"), 1)
                norm(2 * l)
                if l == 0:
                    pool.wait_ge(S("h_ready"), 2)
                    load_norm(1)
                    tables(1)
                    rotations(1)
                    norm(1)
                else:
                    load_norm(2 * l + 1)
                    for tb in range(TB):
                        pool.wait_ge(S("ht_l"), tb + 1)
                        pool.tensor_scalar(h_t[:, tb, :], h_t[:, tb, :], ALPHA, 0.0, ALU.mult, ALU.add
                                           ).then_inc(S("h_scaled"), 1)
            norm(2 * DEPTH - 1)

        @block.scalar
        def _(act):
            link = Link(act, "act_link")

            def evac(dst, label, part=None, last=True, func=ACT.Copy, scale=1.0, bias=0.0):
                src = full(act, *label)
                src = src if part is None else part(src)
                ins = act.activation(dst, src, func, scale=scale, bias=bias)
                if last:
                    ins.then_inc(bank_free[plan[label][0]], 1)
                return ins

            def ssm_exps(l):
                act.wait_ge(S("lam_in"), 64 * LAYER(l))
                act.activation(sc[:, 0, :], lam[:, 2, :], ACT.Exp).then_inc(S("dt"), 1)
                act.wait_ge(S("expo"), LAYER(l))
                act.activation(mag, sc[:, 1, :], ACT.Exp).then_inc(S("mag"), 1)
                act.wait_ge(S("angle"), LAYER(l))
                act.activation(sc[:, 6, :], sc[:, 4, :], ACT.Sin).then_inc(S("sines"), 1)
                act.activation(sc[:, 7, :], sc[:, 5, :], ACT.Sin).then_inc(S("sines"), 1)

            def hi(name):
                n, m = job_at[name], split_at[name]
                act.wait_ge(raw_full[n % RAW], full_value[n])
                if m >= SPLIT:
                    act.wait_ge(S("split_free"), m - SPLIT + 1)
                act.activation(whi[m % SPLIT], raw[n % RAW], ACT.Copy).then_inc(S("hi_full"), 1)

            def hi_e(x, kind, g, half, ahead=0):
                j = moe_at[kind, g, half] + ahead * N_MOE
                s, turn = moe_slot(j)
                act.wait_ge(raw_full[s], x.it * (16 * PER_SLOT) + (filled[s] + 16 * (turn + 1)))
                act.wait_ge(S("split_free"), x.it * N_MOE + (N_SPLIT + j - SPLIT + 1))
                act.activation(whi[(N_SPLIT + j) % SPLIT], raw[s], ACT.Copy).then_inc(S("hi_full"), 1)

            for g in range(4):
                tb, kk = divmod(g, 2)
                evac(hT[:, 4 * kk:4 * kk + 4, tb * P:(tb + 1) * P], ("xT", g), by(P))
            ssm_exps(0)
            for l in range(DEPTH):
                L = LAYER(l)
                for tb in range(TB):
                    act.activation(hre[:, tb, :], by(256)(full(act, "cq", l))[:, tb, :], ACT.Square,
                                   accum_out=MS[:, tb:tb + 1]).then_inc(S("squares"), 1)
                for tb in range(TB):
                    act.activation(him[:, tb, 0:128], by(256)(full(act, "kvi", l))[:, tb, 0:128], ACT.Square,
                                   accum_out=MS[:, 2 + tb:3 + tb]).then_inc(S("squares"), 1)
                for r in range(2):
                    evac(cqs[:, :, 384 + 64 * r:448 + 64 * r], ("kvi", l), lambda b: by(256)(b)[:, :, 128:192], last=False)
                act.activation(widx, by(256)(full(act, "kvi", l))[:, :, 192:196], ACT.Copy,
                               scale=IH ** -0.5 * 64 ** -0.5).then_inc(S("kid"), 1)
                evac(uT, ("u", l), by(256))
                evac(hq, ("hq", l), by(256))
                evac(hP, ("hf", l), by(256), last=False, func=ACT.Sigmoid)
                evac(hk, ("hf", l), by(256), func=ACT.Sigmoid, scale=-1.0)
                if l > 0:
                    act.wait_ge(S("lb_diff"), 1)
                    act.activation(scol[:, 7:9], lbl[:, 1, :], ACT.Sigmoid).then_inc(S("lb_sig"), 1)
                evac(hv, ("hv", l), by(256))
                act.activation(hgs, by(256)(full(act, "hg", l)), ACT.Sigmoid).then_inc(S("hg_sig"), 1)
                evac(bbT.rearrange("p a b n -> p (a b n)"), ("bt", l))
                evac(ccT[:, 0].rearrange("p b n -> p (b n)"), ("cct", l), lambda b: b[:, 0:256], last=False)
                evac(ccT[:, 1].rearrange("p b n -> p (b n)"), ("cct", l), lambda b: b[:, 256:512], scale=-1.0)
                act.wait_ge(S("col_in"), 112 * L)
                for f in range(2):
                    evac(cT[:, f, :], ("cqT", l), lambda b: b[:, 256 * f:256 * f + 256], last=f == 1,
                         scale=scol[:, 4 + f:5 + f])
                evac(cT[:, 2, :], ("kviT", l), lambda b: b[:, 0:256], last=False, scale=scol[:, 6:7])
                evac(cT[:, 3, :], ("kviT", l), lambda b: b[:, 256:512])

                def gate(c):
                    evac(gates[:, 2 * c:2 * c + 2, :], ("gate", l, c), by(256), func=ACT.Sigmoid)

                gate(0)
                for i in range(2):
                    evac(qT[:, 2 * i:2 * i + 2, :], ("q", l, i), by(256), scale=AD ** -0.5)
                evac(qiT, ("qi", l), by(256))
                for i in range(2):
                    evac(kT[:, 2 * i:2 * i + 2, :], ("k", l, i), by(256))
                for tb in range(TB):
                    evac(v_at[:, tb, :], ("v", l, tb))
                gate(1)
                for i in range(4):
                    n = 2 * P if i < 2 else 2 * T
                    o = 256 * i if i < 2 else 512 * (i - 1)
                    evac(relu_s[:, o:o + n], ("idx", l, i), lambda b: b[:, 0:n], func=ACT.Relu)
                for c in range(2, 6):
                    gate(c)
                for tb in range(TB):
                    act.wait_ge(S("row_max"), 2 * l + tb + 1)
                    for h in range(AH):
                        c = tb * AH + h
                        act.activation(probs[tb][:, h, :], probs[tb][:, h, :], ACT.Exp, bias=nmax[:, c:c + 1],
                                       accum_out=psumv[:, c:c + 1]).then_inc(S("probs"), 1)
                for c in range(6, 9):
                    gate(c)
                act.wait_ge(S("h_att_zero"), L)
                for odd in range(2):
                    evac(h_att[:, 2].rearrange("p (a odd) t -> p a odd t", odd=2)[:, :, odd, :], ("lev", l, 8, odd),
                         lambda b: by(P)(b)[:, 0:2, :])
                for i in (0, 2, 4):
                    if i == 4:
                        full(act, "o", l, 0)
                    evac(pT_part(i), ("pT", l, i), by(P))
                act.activation(lq[0].rearrange("p a n -> p (a n)"), full(act, "ho", l), ACT.Square).then_inc(S("ho_sq"), 1)
                gate(9)
                for i in range(2):
                    evac(oT[:, 2 * i:2 * i + 2, :], ("oT", l, i), by(256))
                gate(10)
                evac(hoT, ("hoT", l), by(256))
                gate(11)
                act.wait_ge(S("gelu_in"), L)
                act.activation(ysig, yg, ACT.Sigmoid, scale=2 * math.sqrt(2 / math.pi)).then_inc(S("gelu_sig"), 1)
                for m in range(2):
                    src = full(act, "glu", l)[:, 256 * m:256 * m + 256]
                    if m == 0:
                        act.wait_ge(S("gelu"), L)
                    ins = act.activation(ysig[:, m, :], src, ACT.Sigmoid, bias=scol[:, 2 + m:3 + m])
                ins.then_inc(bank_free[plan[("glu", l)][0]], 1)
                full(act, "y", l, 0, 3)
                hi(("fg", 0)) if l == 0 else hi_e(Expert(0, None), "g", 0, 0)
                full(act, "wo", l, 3)
                if l == 0:
                    hi(("fu", 0))
                    for g in range(4):
                        tb, kk = divmod(g, 2)
                        act.activation(xh[:, 4 * kk:4 * kk + 4, tb * P:(tb + 1) * P], by(P)(full(act, "hT", 0, 0, g)),
                                       ACT.Copy).then_inc(S("xh"), 1)
                    for c in range(CH_FFN):
                        if c == 3:
                            ssm_exps(1)
                        if c + 1 < CH_FFN:
                            hi(("fg", c + 1)), hi(("fu", c + 1))
                        act.activation(a_f[c % 2].rearrange("p a n -> p (a n)"), full(act, "fg", c), ACT.Silu
                                       ).then_inc(bank_free[c % 2], 1)
                        hi(("fd", c))
                        taken(act, "fu", c)
                        act.activation(a_h[c % 2], a_f[c % 2], ACT.Copy).then_inc(S("ffn_ah"), 1)
                    for g in range(4):
                        tb, kk = divmod(g, 2)
                        evac(hT[:, 4 * kk:4 * kk + 4, tb * P:(tb + 1) * P], ("hT", 0, 1, g), by(P))
                else:
                    hi_e(Expert(0, None), "g", 0, 1), hi_e(Expert(0, None), "u", 0, 0)
                    for g in range(4):
                        tb, kk = divmod(g, 2)
                        evac(hTr[:, 4 * kk:4 * kk + 4, tb * P:(tb + 1) * P], ("hT", 1, 0, g), by(P))
                    for tb in range(TB):
                        act.activation(ht_h[:, tb, :], h_t[:, tb, :], ACT.Copy).then_inc(S("ht_h"), 1)
                    act.wait_ge(S("top_diff"), 1)
                    act.activation(rs[:, 6, :], rs[:, 5, :], ACT.Exp).then_inc(S("top_exp"), 1)

            def evac_e(x, dst, *label, src=lambda b: b[:, :], func=ACT.Copy, frees=True):
                ins = act.activation(dst, src(x.full(act, *label)), func)
                ins.then_inc(bank_free[x.at(*label)[0]] if frees else S("et_h"), 1)

            def gathered(x):
                evac_e(x, xe_h[:, 0:4, :], "xe", 0, src=by(P))
                evac_e(x, xe_l[:, 0:4, :], "xe", 2, src=by(P))

            def pass_start(x):
                gathered(x)
                if x.second:
                    hi_e(x, "g", 0, 0), hi_e(x, "g", 0, 1), hi_e(x, "u", 0, 0)

            def expert(x):
                hi_e(x, "u", 0, 1)
                for g in range(GR_MOE):
                    more = g + 1 < GR_MOE
                    if more:
                        hi_e(x, "g", g + 1, 0), hi_e(x, "g", g + 1, 1)
                    evac_e(x, ea[g % 2], "g", g, func=ACT.Silu)
                    if more:
                        hi_e(x, "u", g + 1, 0), hi_e(x, "u", g + 1, 1)
                        if g == 0:
                            evac_e(x, selT, "selT", src=lambda b: b[:, 0:TB * P].rearrange("p (a n) -> p a n", n=P))
                        evac_e(x, et_h[g % 2], "t", g, src=by(P), frees=False)
                        hi_e(x, "d", g, 0), hi_e(x, "d", g, 1)
                    else:
                        hi_e(x, "d", g, 0), hi_e(x, "d", g, 1)
                        evac_e(x, et_h[g % 2], "t", g, src=by(P), frees=False)
                if not x.last:
                    gathered(x)
                    hi_e(x, "g", 0, 0, ahead=1), hi_e(x, "g", 0, 1, ahead=1)
                evac_e(x, y_e[:, 0:512], "y", 0)
                evac_e(x, y_e[:, 512:1024], "y", 1)
                if not x.last:
                    hi_e(x, "u", 0, 0, ahead=1)

            run_pass(act, 0, pass_start, expert)
            act.wait_ge(S("over_ready"), 1)
            with act.If(act.value_load(over_i[0:1, 0:1], min_val=0, max_val=T) > CAP):
                run_pass(act, 1, pass_start, expert)

        @block.tensor
        def _(pe):
            owed = []

            def mm(dst, lhs, rhs, start, stop):
                ins = pe.matmul(dst, lhs, rhs, start=start, stop=stop)
                if owed:
                    ins.then_inc(S("split_free"), 1)
                    owed.clear()
                return ins

            def bank_for(*label):
                b, n = plan[label]
                if n > 0:
                    pe.wait_ge(bank_free[b], n)
                return bank[b]

            def done(ins, *label):
                ins.then_inc(bank_full[plan[label][0]], 1)

            def chunk(name):
                n = job_at[name]
                pe.wait_ge(raw_full[n % RAW], full_value[n])
                return raw[n % RAW]

            def by_token(name, label, n, lhs):
                w = chunk(name)[:, 0:KD * n].rearrange("p (k n) -> p k n", k=KD)
                b = bank_for(*label)
                for tb in range(TB):
                    for k in range(KD):
                        ins = mm(b[:, 256 * tb:256 * tb + n], lhs[:, k, tb * P:(tb + 1) * P], w[:, k, :],
                                 k == 0, k == KD - 1)
                done(ins, *label)

            def by_column(name, label):
                w = chunk(name).rearrange("p (k n) -> p k n", k=KD)
                b = bank_for(*label)
                for m in range(2):
                    for k in range(KD):
                        ins = mm(b[:, 256 * m:256 * m + 256], w[:, k, m * P:(m + 1) * P], hT[:, k, :],
                                 k == 0, k == KD - 1)
                done(ins, *label)

            def transposes(label, sources):
                b = bank_for(*label)
                for i, src in enumerate(sources):
                    ins = pe.transpose(b[0:src.shape[1], i * P:(i + 1) * P], src, ident)
                done(ins, *label)

            pe.wait_ge(S("consts"), 4)
            pe.wait_ge(S("x_in"), 32)
            for g in range(4):
                tb, kk = divmod(g, 2)
                transposes(("xT", g), [h_t[:, tb, P * k:P * (k + 1)] for k in range(4 * kk, 4 * kk + 4)])
            for l in range(DEPTH):
                L = LAYER(l)
                if l == 0:
                    for g in range(4):
                        taken(pe, "xT", g)
                else:
                    for g in range(4):
                        taken(pe, "hT", 0, 1, g)

                def gate(c):
                    by_column(("gate", l, c), ("gate", l, c))

                for name, n in (("cq", 256), ("kvi", N_KVI)):
                    by_token((name, l), (name, l), n, hT)
                for name in ("u", "hq", "hf"):
                    by_column((name, l), (name, l))
                for name in ("hv", "hg"):
                    by_token((name, l), (name, l), 256, hT)
                pe.wait_ge(S("b_exp_ready"), L)
                transposes(("bt", l), [b_exp[:, ri, 4 * m:4 * m + 4, :].rearrange("p j c -> p (j c)")
                                       for ri in range(2) for m in range(2)])
                pe.wait_ge(S("c_exp"), 4 * L)
                transposes(("cct", l), [c_exp[:, ri, m, :] for ri in range(2) for m in range(2)])
                taken(pe, "cq", l)
                taken(pe, "kvi", l)
                transposes(("cqT", l), [cqs[:, tb, P * f:P * f + P] for f in range(2) for tb in range(TB)])
                transposes(("kviT", l), [cqs[:, tb, P * f:P * f + P] for f in range(2, 4) for tb in range(TB)])
                gate(0)
                taken(pe, "cqT", l)
                w = chunk(("uq", l))
                uq, qidx = w[:, 0:1024].rearrange("p (k n) -> p k n", k=2), w[:, 1024:1536].rearrange("p (k n) -> p k n", k=2)
                for i in range(3):
                    label = ("q", l, i) if i < 2 else ("qi", l)
                    b = bank_for(*label)
                    for m in range(2):
                        for k in range(2):
                            lhs = uq[:, k, P * (2 * i + m):P * (2 * i + m + 1)] if i < 2 else qidx[:, k, P * m:P * m + P]
                            ins = mm(b[:, 256 * m:256 * m + 256], lhs, cT[:, k, :], k == 0, k == 1)
                    done(ins, *label)
                taken(pe, "kviT", l)
                ukv = chunk(("ukv", l))
                for i in range(2):
                    b = bank_for("k", l, i)
                    for m in range(2):
                        ins = mm(b[:, 256 * m:256 * m + 256], ukv[:, P * (2 * i + m):P * (2 * i + m + 1)], cT[:, 2, :],
                                 True, True)
                    done(ins, "k", l, i)
                for tb in range(TB):
                    ins = mm(bank_for("v", l, tb)[:, :], cT[:, 2, tb * P:(tb + 1) * P], ukv[:, 512:1024], True, True)
                    done(ins, "v", l, tb)
                gate(1)
                taken(pe, "qi", l)

                def head(ap, h):
                    return ap[64 * (h % 2):64 * (h % 2) + 64, h // 2]

                for i in range(4):
                    b = bank_for("idx", l, i)
                    tb, odd = divmod(i, 2)
                    keys = P * (tb + 1)
                    for j in range(2):
                        ins = mm(b[:, keys * j:keys * (j + 1)], head(qiT, 2 * j + odd)[:, tb * P:(tb + 1) * P],
                                 cT[64 * odd:64 * odd + 64, 3, 0:keys], True, True)
                    done(ins, "idx", l, i)
                gate(2), gate(3)
                taken(pe, "k", l, 1)
                for i in range(6):
                    b = bank_for("lg", l, i)
                    for j in range(4 if i < 2 else 2):
                        h = 2 * j + i if i < 2 else 4 * ((i - 2) // 2) + 2 * j + i % 2
                        keys, tb = (P, 0) if i < 2 else (T, 1)
                        ins = mm(b[:, keys * j:keys * (j + 1)], head(qT, h)[:, tb * P:(tb + 1) * P],
                                 head(kT, h)[:, 0:keys], True, True)
                    done(ins, "lg", l, i)
                gate(4), gate(5)
                for lv in range(9):
                    pe.wait_ge(S("lev_qk"), 9 * l + lv + 1)
                    q_, k_ = (hq, hk) if lv == 0 else (lq[lv % 2], lk[lv % 2])
                    for odd in range(2):
                        b = bank_for("lev", l, lv, odd)
                        for a in range(4 if lv < 8 else 2):
                            h = 2 * (a % 2) + odd
                            qb, kb = (a // 2, a // 2) if lv < 8 else (1, 0)
                            ins = mm(b[:, P * a:P * a + P], head(k_, h)[:, kb * P:(kb + 1) * P],
                                     head(q_, h)[:, qb * P:(qb + 1) * P], True, True)
                        done(ins, "lev", l, lv, odd)
                    if lv in (2, 4, 6):
                        gate(5 + lv // 2)
                for i in range(6):
                    pe.wait_ge(S("probs"), 16 * l + (8 if i < 2 else 16))
                    tb, kb, hg = (0, 0, i) if i < 2 else (1, (1, 0)[i // 2 - 1], i % 2)
                    transposes(("pT", l, i), [probs[tb][:, 4 * hg + j, kb * P:(kb + 1) * P] for j in range(4)])
                    if i == 1:
                        for n in range(2):
                            taken(pe, "pT", l, n)
                        b = bank_for("o", l, 0)
                        for h in range(AH):
                            ins = mm(b[:, AD * h:AD * h + AD], pT[:, 0, h, :], v_at[:, 0, AD * h:AD * h + AD], True, True)
                        done(ins, "o", l, 0)
                for n in range(2, 6):
                    taken(pe, "pT", l, n)
                b = bank_for("o", l, 1)
                for h in range(AH):
                    for kb in (0, 1):
                        ins = mm(b[:, AD * h:AD * h + AD], pT[:, kb, h, :], v_at[:, kb, AD * h:AD * h + AD],
                                 kb == 0, kb == 1)
                done(ins, "o", l, 1)
                taken(pe, "lev", l, 8, 0)
                taken(pe, "lev", l, 8, 1)
                taken(pe, "lev", l, 7, 0)
                taken(pe, "lev", l, 7, 1)
                b = bank_for("ho", l)
                for tb in range(TB):
                    for h in range(HG_H):
                        dst = b[:, 256 * tb + 64 * h:256 * tb + 64 * h + 64]
                        if tb == 1:
                            mm(dst, h_att[:, 2, h, :], hv[:, 0, 64 * h:64 * h + 64], True, False)
                        ins = mm(dst, h_att[:, tb, h, :], hv[:, tb, 64 * h:64 * h + 64], tb == 0, True)
                done(ins, "ho", l)
                def ssm_in(pr):
                    for ri in range(2):
                        b = bank_for("bu", l, pr, ri)
                        rows = slice(32 * pr, 32 * pr + 32)
                        for m in range(2):
                            ins = pe.matmul(b[:, 256 * m:256 * m + 256], bbT[rows, ri, m, :], uT[rows, m, :],
                                            start=True, stop=True, tile_position=(32 * pr, 0))
                        done(ins, "bu", l, pr, ri)

                def ssm_out(pr):
                    pe.wait_ge(S("states"), 2 * (4 * l + pr + 1))
                    b = bank[plan[("ssy", l)][0]] if pr > 0 else bank_for("ssy", l)
                    rows = slice(32 * pr, 32 * pr + 32)
                    for m in range(2):
                        for ri, st in enumerate((hre, him)):
                            ins = pe.matmul(b[rows, 256 * m:256 * m + 256], ccT[:, ri, m, rows], st[:, m, :],
                                            start=(ri == 0), stop=(ri == 1), tile_position=(0, 32 * pr))
                    ins.then_inc(S("states_used") if pr < 3 else bank_full[plan[("ssy", l)][0]], 1)

                ssm_in(0)
                gate(9)
                ssm_in(1)
                taken(pe, "o", l, 1)
                for i in range(2):
                    transposes(("oT", l, i), [o_at[:, tb, P * f:P * f + P] for f in (2 * i, 2 * i + 1) for tb in range(TB)])
                gate(10)
                ssm_out(0)
                ssm_in(2)
                pe.wait_ge(S("ho_ready"), L)
                transposes(("hoT", l), [ho[:, tb, P * f:P * f + P] for f in range(2) for tb in range(TB)])
                gate(11)
                ssm_out(1)
                ssm_in(3)

                def y_out(br, src, names, quarters=range(4)):
                    w = [chunk(n).rearrange("p (k n) -> p k n", k=2) for n in names]
                    nk = 2 * len(names)
                    for q in quarters:
                        b = bank_for("y", l, br, q)
                        for m in range(2):
                            for k in range(nk):
                                ins = mm(b[:, 256 * m:256 * m + 256],
                                         w[k // 2][:, k % 2, P * (2 * q + m):P * (2 * q + m + 1)], src[:, k, :],
                                         k == 0, k == nk - 1)
                        done(ins, "y", l, br, q)

                taken(pe, "hoT", l)
                y_out(1, hoT, [("wout", l, 1)])
                ssm_out(2)
                taken(pe, "oT", l, 1)
                y_out(2, oT, [("wout", l, 2, 0), ("wout", l, 2, 1)], (0, 1))
                ssm_out(3)
                y_out(2, oT, [("wout", l, 2, 0), ("wout", l, 2, 1)], (2, 3))
                pe.wait_ge(S("gelu"), L)
                w = chunk(("glu", l))[:, 0:512].rearrange("p (k n) -> p k n", k=2)
                b = bank_for("glu", l)
                for m in range(2):
                    for k in range(2):
                        ins = mm(b[:, 256 * m:256 * m + 256], w[:, k, P * m:P * m + P], yg[:, k, :], k == 0, k == 1)
                done(ins, "glu", l)
                pe.wait_ge(S("ssm_out"), L)
                y_out(0, ys, [("wout", l, 0)])

                def mixed_ready(k):
                    if k % 2 == 0:
                        pe.wait_ge(S("mixed"), 4 * l + k // 2 + 1)

                for i in range(4):
                    pr, tb = divmod(i, 2)
                    b = bank_for("wo", l, i)
                    for c in range(2):
                        w = chunk(("wo", l, 2 * pr + c)).rearrange("p (k n) -> p k n", k=KD)
                        for k in range(KD):
                            if i == 0 and c == 0:
                                mixed_ready(k)
                            ins = mm(b[:, 256 * c:256 * c + 256], gates[:, k, tb * P:(tb + 1) * P], w[:, k, :],
                                     k == 0, k == KD - 1)
                    done(ins, "wo", l, i)
                for g in range(4):
                    tb, kk = divmod(g, 2)
                    pe.wait_ge(S("h_ready"), 4 * l + tb + 1)
                    transposes(("hT", l, 0, g), [h_t[:, tb, P * k:P * (k + 1)] for k in range(4 * kk, 4 * kk + 4)])
                if l == 0:
                    for g in range(4):
                        taken(pe, "hT", 0, 0, g)

                    def split_chunk(name):
                        m = split_at[name]
                        pe.wait_ge(S("lo_full"), m + 1)
                        return whi[m % SPLIT], wlo[m % SPLIT]

                    def up(kind, c):
                        wh, wl = (w.rearrange("p (k n) -> p k n", k=KD) for w in split_chunk((kind, c)))
                        b = bank_for(kind, c)
                        for m in range(2):
                            for k in range(KD):
                                dst, cs = b[:, 256 * m:256 * m + 256], slice(m * P, (m + 1) * P)
                                mm(dst, wh[:, k, cs], xh[:, k, :], k == 0, False)
                                mm(dst, wh[:, k, cs], xl[:, k, :], False, False)
                                ins = mm(dst, wl[:, k, cs], xh[:, k, :], False, k == KD - 1)
                        done(ins, kind, c)
                        owed.append(1)

                    def down(c):
                        pe.wait_ge(S("ffn_al"), c + 1)
                        wh, wl = (w.rearrange("p (k n) -> p k n", k=2) for w in split_chunk(("fd", c)))
                        for tb in range(TB):
                            for hf in range(2):
                                b = bank_for("fd", tb, hf) if c == 0 else bank[4 + 2 * tb + hf]
                                for k in range(2):
                                    ts, ds = slice(tb * P, (tb + 1) * P), slice(512 * hf, 512 * hf + 512)
                                    mm(b[:, :], a_h[c % 2][:, k, ts], wh[:, k, ds], c == 0 and k == 0, False)
                                    mm(b[:, :], a_l[c % 2][:, k, ts], wh[:, k, ds], False, False)
                                    ins = mm(b[:, :], a_h[c % 2][:, k, ts], wl[:, k, ds], False,
                                             c == CH_FFN - 1 and k == 1)
                                if c == CH_FFN - 1:
                                    done(ins, "fd", tb, hf)
                        owed.append(1)

                    up("fg", 0), up("fu", 0)
                    for c in range(CH_FFN):
                        if c + 1 < CH_FFN:
                            up("fg", c + 1), up("fu", c + 1)
                        down(c)
                    for g in range(4):
                        tb, kk = divmod(g, 2)
                        pe.wait_ge(S("h_ready"), 2 + tb + 1)
                        transposes(("hT", 0, 1, g), [h_t[:, tb, P * k:P * (k + 1)] for k in range(4 * kk, 4 * kk + 4)])
                    owed.clear()
                    pe.sem_inc(S("split_free"), 1)
                else:
                    pe.wait_ge(S("router_in"), 16)
                    b = bank_for("router")
                    for tb in range(TB):
                        for k in range(KD):
                            if k % 4 == 0:
                                taken(pe, "hT", 1, 0, 2 * tb + k // 4)
                            ins = mm(b[:, NE * tb:NE * tb + NE], hTr[:, k, tb * P:(tb + 1) * P], wrt[:, k, :],
                                     k == 0, k == KD - 1)
                    done(ins, "router")
                    pe.wait_ge(S("routed"), 1)
                    b = bank_for("rank")
                    mm(b[:, 0:NE], tri, rt[:, 4, 0, :], True, True)
                    mm(b[:, NE:2 * NE], ones, rt[:, 4, 0, :], True, False)
                    mm(b[:, NE:2 * NE], tri, rt[:, 4, 1, :], False, True)
                    mm(b[:, 2 * NE:3 * NE], ones, rt[:, 4, 0, :], True, False)
                    done(mm(b[:, 2 * NE:3 * NE], ones, rt[:, 4, 1, :], False, True), "rank")

            def room_e(x, *label):
                b, n = x.at(*label)
                pe.wait_ge(bank_free[b], n)
                return bank[b]

            def done_e(x, ins, *label):
                ins.then_inc(bank_full[x.at(*label)[0]], 1)

            def halves(x, kind, g, half, ahead=0):
                j = moe_at[kind, g, half] + ahead * N_MOE
                pe.wait_ge(S("lo_full"), x.it * N_MOE + (N_SPLIT + j + 1))
                m = (N_SPLIT + j) % SPLIT
                return whi[m], wlo[m]

            def gather(x, sel_made):
                pe.wait_ge(S("sel"), sel_made)
                for i in range(4):
                    src, kk = (ht_h, ht_l)[i // 2], 4 * (i % 2)
                    b = room_e(x, "xe", i)
                    for k in range(4):
                        for tb in range(TB):
                            ins = pe.matmul(b[:, P * k:P * k + CAP], src[:, tb, P * (kk + k):P * (kk + k + 1)],
                                            sel[:, tb, :], start=tb == 0, stop=tb == TB - 1)
                    done_e(x, ins, "xe", i)

            def up_half(x, kind, g, half, b, ahead=0):
                wh, wl = (w.rearrange("p (k n) -> p k n", k=4) for w in halves(x, kind, g, half, ahead))
                for k in range(4):
                    x_h, x_l = xe_h[:, 4 * half + k, :], xe_l[:, 4 * half + k, :]
                    mm(b[0:CAP, :], x_h, wh[:, k, :], half == 0 and k == 0, False)
                    mm(b[0:CAP, :], x_l, wh[:, k, :], False, False)
                    ins = mm(b[0:CAP, :], x_h, wl[:, k, :], False, half == 1 and k == 3)
                owed.append(1)
                return ins

            def up_e(x, kind, g):
                b = room_e(x, kind, g)
                up_half(x, kind, g, 0, b)
                done_e(x, up_half(x, kind, g, 1, b), kind, g)

            def down_e(x, g):
                x.taken(pe, "t", g)
                ys_ = [room_e(x, "y", i) for i in range(2)] if g == 0 else [bank[4], bank[5]]
                for half in range(2):
                    wh, wl = (w.rearrange("p (k n) -> p k n", k=2) for w in halves(x, "d", g, half))
                    for i in range(2):
                        for k in range(2):
                            eh, el = et_h[g % 2][:, 2 * half + k, :], et_l[g % 2][:, 2 * half + k, :]
                            cs = slice(512 * i, 512 * i + 512)
                            first_ = g == 0 and half == 0 and k == 0
                            last_ = g == GR_MOE - 1 and half == 1 and k == 1
                            mm(ys_[i][0:CAP, :], eh, wh[:, k, cs], first_, False)
                            mm(ys_[i][0:CAP, :], el, wh[:, k, cs], False, False)
                            ins = mm(ys_[i][0:CAP, :], eh, wl[:, k, cs], False, last_)
                        if g == GR_MOE - 1 and half == 1:
                            done_e(x, ins, "y", i)
                    owed.append(1)

            def pass_start(x):
                gather(x, 1 if x.second == 0 else NE + 2)
                for i in range(4):
                    x.taken(pe, "xe", i)
                b, n = Expert(x.second, 0).at("g", 0)
                pe.wait_ge(bank_free[b], n)
                up_half(x, "g", 0, 0, bank[b])
                assert owed

            def expert(x):
                done_e(x, up_half(x, "g", 0, 1, bank[x.at("g", 0)[0]]), "g", 0)
                up_e(x, "u", 0)
                for g in range(GR_MOE):
                    if g + 1 < GR_MOE:
                        up_e(x, "g", g + 1)
                    if g == 0:
                        b = room_e(x, "selT")
                        for tb in range(TB):
                            ins = pe.transpose(b[:, tb * P:(tb + 1) * P], selg[:, tb, :], ident)
                        done_e(x, ins, "selT")
                    x.taken(pe, "u", g)
                    b = room_e(x, "t", g)
                    for f in range(4):
                        ins = pe.transpose(b[:, P * f:P * f + CAP], ea[g % 2][:, P * f:P * f + P], ident)
                    done_e(x, ins, "t", g)
                    if g + 1 < GR_MOE:
                        up_e(x, "u", g + 1)
                    elif not x.last:
                        gather(x, x.it + (2 + x.second))
                    down_e(x, g)
                if not x.last:
                    for i in range(4):
                        x.taken(pe, "xe", i)
                    b, n = Expert(x.second, x.e).at("g", 0)
                    pe.wait_ge(bank_free[b], n + body_uses[b])
                    up_half(x, "g", 0, 0, bank[b], ahead=1)
                x.taken(pe, "y", 0), x.taken(pe, "y", 1)
                for q in range(4):
                    tb, hf = divmod(q, 2)
                    b = room_e(x, "sc", q)
                    done_e(x, pe.matmul(b[:, :], selT[:, tb, :], y_e[:, 512 * hf:512 * hf + 512], start=True, stop=True),
                           "sc", q)
                assert owed

            run_pass(pe, 0, pass_start, expert)
            pe.wait_ge(S("over_ready"), 1)
            with pe.If(pe.value_load(over_i[0:1, 0:1], min_val=0, max_val=T) > CAP):
                run_pass(pe, 1, pass_start, expert)

        @block.vector
        def _(dve):
            link = Link(dve, "dve_link")

            dve.wait_ge(S("c0"), 10)
            lev, below, cmp_ = score[:, 0:P], score[:, P:2 * P], work[:, 0:P]
            link(dve.tensor_copy(par_i, ip[:, 0:2]))
            link(dve.tensor_tensor(cmp_, jf, ip, ALU.is_gt))
            link(dve.tensor_tensor(ip, ip, jf, ALU.bitwise_xor))
            link(dve.tensor_copy(lev, ip))
            link(dve.tensor_scalar(lev_mask[:, 0, :], lev, 0.0, None, ALU.is_equal))
            link(dve.tensor_tensor(lev, lev, cmp_, ALU.mult))
            for j in range(7):
                link(dve.tensor_scalar(below, lev, float(2 << j), None, ALU.is_lt))
                link(dve.scalar_tensor_tensor(lev_mask[:, j + 1, :], lev, float(1 << j), below, ALU.is_ge, ALU.mult))
            link(dve.tensor_scalar(par_i, par_i, 4, 1, ALU.logical_shift_right, ALU.bitwise_and))
            link(dve.tensor_copy(par[:, 1:2], par_i[:, 0:1]))
            dve.tensor_scalar(par[:, 0:1], par[:, 1:2], -1.0, 1.0, ALU.mult, ALU.add).then_inc(S("par"), 1)
            link(dve.memset(scol[:, 7:9], 0.0))
            link(dve.memset(scol[:, 9:11], 1.0))

            def taken_by(b_label, ins):
                ins.then_inc(bank_free[plan[b_label][0]], 1)
                taken(dve, *b_label)

            def lo(name):
                n, m = job_at[name], split_at[name]
                dve.wait_ge(S("hi_full"), m + 1)
                dve.tensor_tensor(wlo[m % SPLIT], raw[n % RAW], whi[m % SPLIT].bitcast(F32), ALU.subtract
                                  ).then_inc(S("lo_full"), 1)

            def lo_e(x, kind, g, half, ahead=0):
                j = moe_at[kind, g, half] + ahead * N_MOE
                m, (s, _) = (N_SPLIT + j) % SPLIT, moe_slot(j)
                dve.wait_ge(S("hi_full"), x.it * N_MOE + (N_SPLIT + j + 1))
                dve.tensor_tensor(wlo[m], raw[s], whi[m].bitcast(F32), ALU.subtract).then_inc(S("lo_full"), 1)

            def norm_stats(tb, hf, order=link):
                order(dve.bn_stats(bn6[:, tb, hf, :], h_t[:, tb, 512 * hf:512 * hf + 512]))

            def layer_norm(n, tb):
                dve.bn_aggr(mv[:, tb, :], bn6[:, tb]).then_inc(S("norm_var"), 1)
                dve.wait_ge(S("norm_in"), 32 * (n + 1))
                dve.wait_ge(S("norm_var"), TB * n + tb + 1)
                link(dve.scalar_tensor_tensor(h_t[:, tb, :], h_t[:, tb, :], mv[:, tb, 0:1], lng[:, 0, :],
                                              ALU.subtract, ALU.mult))
                dve.wait_ge(S("norm_rstd"), TB * n + tb + 1)
                dve.scalar_tensor_tensor(h_t[:, tb, :], h_t[:, tb, :], rstd[:, tb:tb + 1], lng[:, 1, :],
                                         ALU.mult, ALU.add).then_inc(S("h_ready"), 1)

            def flat(ap):
                return ap.rearrange("p a t -> p (a t)")

            for l in range(DEPTH):
                L = LAYER(l)
                dve.wait_ge(S("rms"), L)
                dve.wait_ge(S("kid"), L)
                cqb, kvb = by(256)(full(dve, "cq", l)), by(256)(full(dve, "kvi", l))
                for tb in range(TB):
                    ins = dve.tensor_scalar(cqs[:, tb, 0:256], cqb[:, tb, :], RMS[:, tb:tb + 1], None, ALU.mult)
                ins.then_inc(bank_free[plan[("cq", l)][0]], 1)
                for tb in range(TB):
                    ins = dve.tensor_scalar(cqs[:, tb, 256:384], kvb[:, tb, 0:128], RMS[:, 2 + tb:3 + tb], None, ALU.mult)
                ins.then_inc(bank_free[plan[("kvi", l)][0]], 1)
                if l > 0:
                    dve.wait_ge(S("col_in"), 112 * L)
                    dve.tensor_tensor(lbl[:, 1, :], lbl[:, 1, :], lbl[:, 0, :], ALU.subtract).then_inc(S("lb_diff"), 1)
                    dve.wait_ge(S("lb_sig"), 1)
                    link(dve.tensor_scalar(scol[:, 9:11], scol[:, 7:9], -1.0, 1.0, ALU.mult, ALU.add))
                taken(dve, "hf", l)
                for m in range(2):
                    link(dve.tensor_scalar(hP[:, m, :], hP[:, m, :], scol[:, 9 + m:10 + m], scol[:, 7 + m:8 + m],
                                           ALU.mult, ALU.add))
                    link(dve.tensor_scalar(hk[:, m, :], hk[:, m, :], scol[:, 9 + m:10 + m], None, ALU.mult))
                link(dve.tensor_scalar(hP, hP, 1e-12, None, ALU.max))
                taken(dve, "hq", l)
                dve.memset(hR, 1.0).then_inc(S("lev_qk"), 1)
                dve.wait_ge(S("hg_sig"), L)
                ins = dve.tensor_tensor(hgs, hgs, by(256)(full(dve, "hg", l)), ALU.mult)
                taken_by(("hg", l), ins)
                dve.wait_ge(S("col_in"), 112 * L)
                hgs8 = hgs.rearrange("p b (h k) -> p (b h) k", k=HG_K)
                link(dve.tensor_tensor(hgs8, hgs8, hgn.unsqueeze(1).to_broadcast((P, 8, HG_K)), ALU.mult))
                dve.wait_ge(S("consts"), 4)
                for tb in range(TB):
                    n = P * (tb + 1)
                    o = P * tb
                    sco, wk, neg = score[:, o:o + n], work[:, o:o + n], negd[:, o:o + n]
                    for h in range(IH):
                        if h < 2:
                            taken(dve, "idx", l, 2 * tb + h)
                        o_h = (h % 2) * 2 * n + (h // 2) * n + 512 * tb
                        src = relu_s[:, o_h:o_h + n]
                        if h == 0:
                            link(dve.tensor_scalar(sco, src, widx[:, tb, 0:1], None, ALU.mult))
                        else:
                            link(dve.scalar_tensor_tensor(sco, src, widx[:, tb, h:h + 1], sco, ALU.mult, ALU.add))
                    link(dve.tensor_scalar(wk, neg, -1e29, MASK, ALU.is_lt, ALU.mult))
                    link(dve.tensor_tensor(sco, sco, wk, ALU.add))
                    src = sco
                    for r in range(N_SEL // 8):
                        link(dve.max(top8, src))
                        link(dve.match_replace(wk, top8, src, TAKEN))
                        src = wk
                    link(dve.tensor_scalar(sco, wk, TAKEN, MASK, ALU.not_equal, ALU.mult))
                    link(dve.tensor_tensor(sco, sco, neg, ALU.add))
                for tb in range(TB):
                    n, o = P * (tb + 1), P * tb
                    for h in range(AH):
                        i, j = (h % 2, h // 2) if tb == 0 else (2 + 2 * (h // 4) + h % 2, h % 4 // 2)
                        label = ("lg", l, i)
                        src = by(n)(full(dve, *label))[:, j, :]
                        ins = dve.scalar_tensor_tensor(probs[tb][:, h, :], score[:, o:o + n], 2.0 ** -(h + 1.0), src,
                                                       ALU.mult, ALU.add)
                        if j == 512 // n - 1:
                            ins.then_inc(bank_free[plan[label][0]], 1)
                    taken(dve, *label)
                    mx = nmax[:, 8 * tb:8 * tb + 8]
                    link(dve.tensor_reduce(mx, probs[tb], AX_X, ALU.max))
                    dve.tensor_scalar(mx, mx, -1.0, None, ALU.mult).then_inc(S("row_max"), 1)
                dve.wait_ge(S("lev_zero"), 2 * L)
                dve.wait_ge(S("h_att_zero"), L)

                def level(lv):
                    n = 1 << (lv - 1)
                    v4 = lambda ap: flat(ap).rearrange("p (b two n) -> p b two n", two=2, n=n)
                    q4, k4, P4, R4 = v4(hq), v4(hk), v4(hP), v4(hR)
                    nb = 512 // (2 * n)
                    dve.tensor_tensor(v4(lq[lv % 2])[:, :, 1, :], q4[:, :, 1, :], P4[:, :, 1, :], ALU.mult)
                    link(dve.tensor_tensor(v4(lk[lv % 2])[:, :, 0, :], k4[:, :, 0, :], R4[:, :, 0, :], ALU.mult))
                    if lv < 8:
                        link(dve.tensor_tensor(R4[:, :, 0, :], R4[:, :, 0, :],
                                               P4[:, :, 1, n - 1:n].to_broadcast((P, nb, n)), ALU.mult))
                        dve.tensor_tensor(P4[:, :, 1, :], P4[:, :, 1, :],
                                          P4[:, :, 0, n - 1:n].to_broadcast((P, nb, n)), ALU.mult
                                          ).then_inc(S("lev_qk"), 1)
                    else:
                        dve.sem_inc(S("lev_qk"), 1)
                    dve.wait_ge(S("lev_qk"), 9 * l + lv + 1)

                for lv in range(8):
                    level(lv + 1)
                    for odd in range(2):
                        dst = h_att[:, 0:2].rearrange("p b (a odd) t -> p (b a) odd t", odd=2)[:, :, odd, :]
                        mask = lev_mask[:, lv, :].unsqueeze(1).to_broadcast((P, 4, P))
                        ins = dve.copy_predicated(dst, mask, by(P)(full(dve, "lev", l, lv, odd)))
                        ins.then_inc(bank_free[plan[("lev", l, lv, odd)][0]], 1)
                for i in (1, 3, 5):
                    if i == 5:
                        full(dve, "o", l, 0)
                    ins = dve.tensor_copy(pT_part(i), by(P)(full(dve, "pT", l, i)))
                    ins.then_inc(bank_free[plan[("pT", l, i)][0]], 1)
                dve.wait_ge(S("probs"), 16 * L)
                link(dve.reciprocal(psumv, psumv))
                for tb in range(TB):
                    b = full(dve, "o", l, tb)
                    ins = dve.tensor_tensor(o_at[:, tb].rearrange("p (h d) -> p h d", d=AD),
                                            b[:, :].rearrange("p (h d) -> p h d", d=AD),
                                            wide(psumv[:, 8 * tb:8 * tb + 8], (P, AH, AD)), ALU.mult)
                    ins.then_inc(bank_free[plan[("o", l, tb)][0]], 1)
                dve.wait_ge(S("ho_sq"), L)
                dve.tensor_reduce(hss, flat(lq[0]).rearrange("p (g k) -> p g k", k=HG_K), AX_X, ALU.add
                                  ).then_inc(S("ho_sum"), 1)
                dve.wait_ge(S("ho_rms"), L)
                ho8 = ho.rearrange("p b (h k) -> p (b h) k", k=HG_K)
                ins = dve.tensor_tensor(ho8, full(dve, "ho", l)[:, :].rearrange("p (g k) -> p g k", k=HG_K),
                                        wide(hrr, (P, 8, HG_K)), ALU.mult)
                taken_by(("ho", l), ins)
                dve.tensor_tensor(ho, ho, hgs, ALU.mult).then_inc(S("ho_ready"), 1)
                dve.wait_ge(S("tables"), L)
                for pr in range(4):
                    ct, st = pair(cos_t, pr), pair(sin_t, pr)
                    gr, gi = xr[pr % 2], xi[pr % 2]
                    if pr >= 2:
                        dve.wait_ge(S("states"), 2 * (4 * l + pr - 1))
                    br, bi = by(256)(full(dve, "bu", l, pr, 0)), by(256)(full(dve, "bu", l, pr, 1))
                    dve.tensor_tensor(sv[0], br, ct, ALU.mult)
                    link(dve.tensor_tensor(sv[1], bi, st, ALU.mult))
                    link(dve.tensor_tensor(gr, sv[0], sv[1], ALU.add))
                    taken_by(("bu", l, pr, 1), dve.tensor_tensor(sv[0], bi, ct, ALU.mult))
                    taken_by(("bu", l, pr, 0), dve.tensor_tensor(sv[1], br, st, ALU.mult))
                    link(dve.tensor_tensor(gi, sv[0], sv[1], ALU.subtract))
                    for g in (gr, gi):
                        for i in range(2):
                            j = pr + 4 * i
                            dve.tensor_tensor_scan(g[:, i, :], mag[:, j:j + 1].to_broadcast((P, T)), g[:, i, :], 0.0,
                                                   ALU.mult, ALU.add).then_inc(S("scan"), 1)

                def mix(br, q):
                    g0 = gates[:, 8 * br + 2 * q:8 * br + 2 * q + 2, :]
                    ins = dve.tensor_tensor(g0, g0, by(256)(full(dve, "y", l, br, q)), ALU.mult)
                    taken_by(("y", l, br, q), ins)
                    return g0

                taken(dve, "gate", l, 11)
                for q in range(4):
                    mix(1, q)
                for q in range(4):
                    if q == 2:
                        b = full(dve, "ssy", l)
                        for m in range(2):
                            ins = dve.scalar_tensor_tensor(ys[:, m, :], uT[:, m, :], scol[:, m:m + 1],
                                                           b[:, 256 * m:256 * m + 256], ALU.mult, ALU.add)
                        ins.then_inc(bank_free[plan[("ssy", l)][0]], 1)
                    g2 = mix(2, q)
                    g1 = gates[:, 8 + 2 * q:8 + 2 * q + 2, :]
                    link(dve.tensor_tensor(g1, g1, g2, ALU.add))
                for q in range(4):
                    g0 = mix(0, q)
                    dve.tensor_tensor(g0, g0, gates[:, 8 + 2 * q:8 + 2 * q + 2, :], ALU.add).then_inc(S("mixed"), 1)
                for i in range(4):
                    pr, tb = divmod(i, 2)
                    hs = h_t[:, tb, 512 * pr:512 * pr + 512]
                    ins = dve.scalar_tensor_tensor(hs, hs, ALPHA, full(dve, "wo", l, i)[:, :], ALU.mult, ALU.add)
                    taken_by(("wo", l, i), ins)
                    norm_stats(tb, pr)
                    if i == 1:
                        lo(("fg", 0)) if l == 0 else lo_e(Expert(0, None), "g", 0, 0)
                    if pr == 1:
                        layer_norm(2 * l, tb)
                if l == 0:
                    for g in range(4):
                        tb, kk = divmod(g, 2)
                        dve.wait_ge(S("xh"), g + 1)
                        part = lambda ap: ap[:, 4 * kk:4 * kk + 4, tb * P:(tb + 1) * P]
                        ins = dve.tensor_tensor(part(xl), by(P)(full(dve, "hT", 0, 0, g)), part(xh).bitcast(F32), ALU.subtract)
                        ins.then_inc(bank_free[plan[("hT", 0, 0, g)][0]], 1)
                    lo(("fu", 0))
                    for c in range(CH_FFN):
                        if c + 1 < CH_FFN:
                            lo(("fg", c + 1)), lo(("fu", c + 1))
                        taken(dve, "fg", c)
                        af = flat(a_f[c % 2])
                        ins = dve.tensor_tensor(af, af, full(dve, "fu", c)[:, :], ALU.mult)
                        taken_by(("fu", c), ins)
                        lo(("fd", c))
                        dve.wait_ge(S("ffn_ah"), c + 1)
                        dve.tensor_tensor(a_l[c % 2], a_f[c % 2], a_h[c % 2].bitcast(F32), ALU.subtract
                                          ).then_inc(S("ffn_al"), 1)
                    for tb in range(TB):
                        for hf in range(2):
                            hs = h_t[:, tb, 512 * hf:512 * hf + 512]
                            ins = dve.scalar_tensor_tensor(hs, hs, ALPHA, full(dve, "fd", tb, hf)[:, :], ALU.mult, ALU.add)
                            taken_by(("fd", tb, hf), ins)
                            norm_stats(tb, hf)
                        layer_norm(1, tb)

            lo_e(Expert(0, None), "g", 0, 1), lo_e(Expert(0, None), "u", 0, 0)
            for g in range(4):
                taken(dve, "hT", 1, 0, g)
            for tb in range(TB):
                dve.wait_ge(S("ht_h"), tb + 1)
                dve.tensor_tensor(ht_l[:, tb, :], h_t[:, tb, :], ht_h[:, tb, :].bitcast(F32), ALU.subtract
                                  ).then_inc(S("ht_l"), 1)
            lgt, oh1, oh2, tmp, msk, rank, gat = (rt[:, i] for i in range(7))
            r8 = over
            link(dve.tensor_scalar(r8, jrow[:, 0:NE], -1.0, float(NE), ALU.mult, ALU.add))
            r8b = r8.unsqueeze(1).to_broadcast((P, TB, NE))
            b = full(dve, "router")
            ins = dve.tensor_copy(lgt, b[:, 0:TB * NE].rearrange("p (b e) -> p b e", e=NE))
            taken_by(("router",), ins)
            src = lgt
            for oh, m in ((oh1, 0), (oh2, 2)):
                link(dve.tensor_reduce(rs[:, m, :], src, AX_X, ALU.max))
                link(dve.tensor_tensor(tmp, src, wide(rs[:, m, :], (P, TB, NE)), ALU.is_equal))
                link(dve.tensor_tensor(tmp, tmp, r8b, ALU.mult))
                link(dve.tensor_reduce(rs[:, m + 1, :], tmp, AX_X, ALU.max))
                link(dve.tensor_tensor(oh, tmp, wide(rs[:, m + 1, :], (P, TB, NE)), ALU.is_equal))
                if m == 0:
                    link(dve.scalar_tensor_tensor(msk, oh, TAKEN, lgt, ALU.mult, ALU.add))
                    src = msk
            dve.tensor_tensor(rs[:, 5, :], rs[:, 2, :], rs[:, 0, :], ALU.subtract).then_inc(S("top_diff"), 1)
            dve.tensor_tensor(msk, oh1, oh2, ALU.add).then_inc(S("routed"), 1)
            dve.wait_ge(S("top_exp"), 1)
            link(dve.tensor_scalar(rs[:, 7, :], rs[:, 6, :], 1.0, None, ALU.add))
            link(dve.reciprocal(rs[:, 7, :], rs[:, 7, :]))
            link(dve.tensor_tensor(rs[:, 8, :], rs[:, 6, :], rs[:, 7, :], ALU.mult))
            link(dve.tensor_tensor(gat, oh1, wide(rs[:, 7, :], (P, TB, NE)), ALU.mult))
            link(dve.tensor_tensor(tmp, oh2, wide(rs[:, 8, :], (P, TB, NE)), ALU.mult))
            link(dve.tensor_tensor(gat, gat, tmp, ALU.add))
            b = full(dve, "rank")
            link(dve.tensor_scalar(rank, b[:, 0:TB * NE].rearrange("p (b e) -> p b e", e=NE), 1.0, None, ALU.add))
            link(dve.tensor_reduce(cur[:, 3:4], b[:, 2 * NE:3 * NE], AX_X, ALU.max))
            link(dve.tensor_tensor(rank, rank, msk, ALU.mult))
            link(dve.tensor_scalar(rank, rank, -1.0, None, ALU.add))
            dve.tensor_copy(over_i, cur[0:1, 3:4]).then_inc(S("over_ready"), 1)
            taken_by(("rank",), dve.memset(cur[:, 0:1], 0.0))

            def select_expert(order):
                order(dve.tensor_scalar(rt[:, 7, 0, :], jrow[:, 0:NE], cur[:, 0:1], None, ALU.is_equal))
                e8 = rt[:, 7, 0, :].unsqueeze(1).to_broadcast((P, TB, NE))
                dve.tensor_tensor(rt[:, 8], rank, e8, ALU.mult)
                order(dve.tensor_tensor(rt[:, 9], gat, e8, ALU.mult))
                dve.tensor_reduce(rs[:, 0, :], rt[:, 8], AX_X, ALU.add)
                order(dve.tensor_reduce(rs[:, 1, :], rt[:, 9], AX_X, ALU.add))
                order(dve.tensor_scalar(cur[:, 0:1], cur[:, 0:1], 1.0, None, ALU.add))

            def select_places(order):
                for tb in range(TB):
                    dve.tensor_scalar(sel[:, tb, :], jrow[:, 0:CAP], rs[:, 0, tb:tb + 1], None, ALU.is_equal)
                    order(dve.tensor_scalar(selg[:, tb, :], jrow[:, 0:CAP], rs[:, 0, tb:tb + 1], rs[:, 1, tb:tb + 1],
                                            ALU.is_equal, ALU.mult))
                dve.sem_inc(S("sel"), 1)

            SEL_LINKS = 6

            def done_e(x, ins, *label):
                ins.then_inc(bank_free[x.at(*label)[0]], 1)

            def gathered(x):
                for i, dst in ((1, xe_h), (3, xe_l)):
                    done_e(x, dve.tensor_copy(dst[:, 4:8, :], by(P)(x.full(dve, "xe", i))), "xe", i)

            def pass_start(x):
                gathered(x)
                if x.second:
                    lo_e(x, "g", 0, 0), lo_e(x, "g", 0, 1), lo_e(x, "u", 0, 0)

            def expert(x):
                order = Link(dve, "dve_loop", start=x.it * SEL_LINKS + 4 * x.second)
                lo_e(x, "u", 0, 1)
                for g in range(GR_MOE):
                    more = g + 1 < GR_MOE
                    if more:
                        lo_e(x, "g", g + 1, 0), lo_e(x, "g", g + 1, 1)
                    x.taken(dve, "g", g)
                    done_e(x, dve.tensor_tensor(ea[g % 2], ea[g % 2], x.full(dve, "u", g)[:, :], ALU.mult), "u", g)
                    for half in range(2):
                        lo_e(x, *(("u", g + 1, half) if more else ("d", g, half)))
                    x_t = x.full(dve, "t", g)
                    dve.wait_ge(S("et_h"), x.it * GR_MOE + (g + 1))
                    done_e(x, dve.tensor_tensor(et_l[g % 2], by(P)(x_t), et_h[g % 2].bitcast(F32), ALU.subtract), "t", g)
                    if more:
                        lo_e(x, "d", g, 0), lo_e(x, "d", g, 1)
                    if g == 2:
                        select_expert(order)
                    if g == 4:
                        select_places(order)
                if not x.last:
                    gathered(x)
                    for kind, half in (("g", 0), ("g", 1), ("u", 0)):
                        lo_e(x, kind, 0, half, ahead=1)
                for q in range(4):
                    tb, hf = divmod(q, 2)
                    hs = h_t[:, tb, 512 * hf:512 * hf + 512]
                    done_e(x, dve.tensor_tensor(hs, hs, x.full(dve, "sc", q)[:, :], ALU.add), "sc", q)
                    if x.last:
                        x.taken(dve, "sc", q)
                        norm_stats(tb, hf, order)
                assert order.n == SEL_LINKS + (4 if x.last else 0)

            select_expert(link), select_places(link)
            dve.wait_ge(S("h_scaled"), TB)
            run_pass(dve, 0, pass_start, expert)
            dve.wait_ge(S("over_ready"), 1)
            with dve.If(dve.value_load(over_i[0:1, 0:1], min_val=0, max_val=T) > CAP):
                again = Link(dve, "dve_again")
                again(dve.tensor_scalar(rank, rank, -float(CAP), None, ALU.add))
                again(dve.memset(cur[:, 0:1], 0.0))
                select_expert(again), select_places(again)
                run_pass(dve, 1, pass_start, expert)
            for tb in range(TB):
                layer_norm(2 * DEPTH - 1, tb)


_INS = ['x', 'w_in', 'ssm_log_dt', 'ssm_lambda_re', 'ssm_lambda_im', 'ssm_b_re', 'ssm_b_im', 'ssm_c_re', 'ssm_c_im',
        'ssm_d', 'ssm_w_glu', 'ssm_b_glu', 'ssm_w_out', 'hgrn_lb_logits', 'hgrn_norm_g', 'hgrn_w_out',
        'attn_q_norm_g', 'attn_kv_norm_g', 'attn_w_uq', 'attn_w_qidx', 'attn_w_ukv', 'attn_w_out', 'w_o',
        'ln_g', 'ln_b', 'ffn_w_gate', 'ffn_w_up', 'ffn_w_down', 'moe_router', 'moe_w_gate', 'moe_w_up', 'moe_w_down']


def kernel(**inputs):
    import numpy as _np
    import concourse.bacc as _bacc
    from concourse import mybir as _mybir
    from concourse.bass_utils import run_bass_kernel_spmd as _run

    nc = _bacc.Bacc("TRN2", target_bir_lowering=False, num_devices=1)
    arrays, args = {}, []
    for name in _INS:
        a = _np.ascontiguousarray(inputs[name])
        arrays[f"in_{name}_dram"] = a
        args.append(nc.dram_tensor(f"in_{name}_dram", a.shape, _mybir.dt.from_np(a.dtype), kind="ExternalInput").ap())
    args.append(nc.dram_tensor("out_0_dram", (1, T, D), F32, kind="ExternalOutput").ap())
    hybrid_kernel(nc, *args)
    r = _run(nc, [arrays], core_ids=[0])
    return r.results[0]["out_0_dram"]
```
